# Optimizing a Trainium2 kernel written in Bass

```python
import jax, jax.numpy as jnp
from jax import lax
import numpy as np

D_MODEL = 1024
BATCH = 1
SEQ = 512
DEPTH = 2

CHUNK = 64
N_MIXERS = 2
EPS = 1e-6

A_HEADS = 16
A_HEAD_DIM = 64
A_KV_HEADS = 2
A_GROUP = A_HEADS // A_KV_HEADS
A_WINDOW = 128
A_WINDOW_CHUNKS = A_WINDOW // CHUNK
ROPE_THETA = 500000.0
ROPE_DIM = A_HEAD_DIM // 4
A_Q_COLS = A_HEADS * A_HEAD_DIM
A_KV_COLS = A_KV_HEADS * A_HEAD_DIM
A_IN_COLS = A_Q_COLS + 2 * A_KV_COLS

R_HEADS = 4
R_QK_DIM = D_MODEL // R_HEADS
R_V_DIM = 2 * D_MODEL // R_HEADS
R_ROT_BASE = 10000.0
R_QK_COLS = R_HEADS * R_QK_DIM
R_V_COLS = R_HEADS * R_V_DIM
R_IN_COLS = 2 * R_QK_COLS + 2 * R_V_COLS

D_FF = 2816
CONV_WIDTH = 3

N_A_LAYERS = (DEPTH + 1) // 2
N_B_LAYERS = DEPTH // 2

kernel_name = "hybrid_swa_sink_retention_convffn"

def rmsnorm(x, g):
    xf = x.astype(jnp.float32)
    y = xf * lax.rsqrt(jnp.mean(xf * xf, axis=-1, keepdims=True) + EPS)
    return (y * g.astype(jnp.float32)).astype(x.dtype)

def rotary(x, pos, base, rot_dim):
    half = rot_dim // 2
    inv_freq = base ** (-jnp.arange(half, dtype=jnp.float32) * 2.0 / rot_dim)
    ang = pos[:, None] * inv_freq[None, :]
    cos = jnp.cos(ang)[:, None, :].astype(x.dtype)
    sin = jnp.sin(ang)[:, None, :].astype(x.dtype)
    x1 = x[..., :half]
    x2 = x[..., half:rot_dim]
    return jnp.concatenate([x1 * cos - x2 * sin, x2 * cos + x1 * sin, x[..., rot_dim:]], axis=-1)

def swa_sink_attention(h, w_qkv, w_o, q_gain, k_gain, sinks):
    B, S, _ = h.shape
    nc = S // CHUNK
    qkv = h @ w_qkv
    q, k, v = jnp.split(qkv, [A_Q_COLS, A_Q_COLS + A_KV_COLS], axis=-1)
    q = q.reshape(B, S, A_HEADS, A_HEAD_DIM)
    k = k.reshape(B, S, A_KV_HEADS, A_HEAD_DIM)
    v = v.reshape(B, S, A_KV_HEADS, A_HEAD_DIM)
    q = rmsnorm(q, q_gain)
    k = rmsnorm(k, k_gain)
    pos = jnp.arange(S, dtype=jnp.float32)
    q = rotary(q, pos, ROPE_THETA, ROPE_DIM)
    k = rotary(k, pos, ROPE_THETA, ROPE_DIM)
    qb = q.reshape(B, nc, CHUNK, A_KV_HEADS, A_GROUP, A_HEAD_DIM)
    pad = A_WINDOW_CHUNKS - 1
    kp = jnp.pad(k.reshape(B, nc, CHUNK, A_KV_HEADS, A_HEAD_DIM), ((0, 0), (pad, 0), (0, 0), (0, 0), (0, 0)))
    vp = jnp.pad(v.reshape(B, nc, CHUNK, A_KV_HEADS, A_HEAD_DIM), ((0, 0), (pad, 0), (0, 0), (0, 0), (0, 0)))
    kb = jnp.concatenate([kp[:, j:j + nc] for j in range(A_WINDOW_CHUNKS)], axis=2)
    vb = jnp.concatenate([vp[:, j:j + nc] for j in range(A_WINDOW_CHUNKS)], axis=2)
    src_chunk = jnp.arange(nc)[:, None] - pad + jnp.arange(A_WINDOW_CHUNKS)[None, :]
    valid = jnp.repeat(src_chunk >= 0, CHUNK, axis=1)
    scores = jnp.einsum('bnqhgd,bnkhd->bnhgqk', qb, kb, preferred_element_type=jnp.float32)
    scores = scores * (A_HEAD_DIM ** -0.5)
    scores = jnp.where(valid[None, :, None, None, None, :], scores, jnp.float32(-1e30))
    sink = sinks.astype(jnp.float32).reshape(A_KV_HEADS, A_GROUP)[None, None, :, :, None, None]
    m = jnp.maximum(jnp.max(scores, axis=-1, keepdims=True), sink)
    p = jnp.exp(scores - m)
    probs = p / (jnp.sum(p, axis=-1, keepdims=True) + jnp.exp(sink - m))
    out = jnp.einsum('bnhgqk,bnkhd->bnqhgd', probs.astype(v.dtype), vb)
    return out.reshape(B, S, A_Q_COLS) @ w_o

def retention(h, w_in, w_o):
    B, S, _ = h.shape
    nc = S // CHUNK
    q, k, v, g = jnp.split(h @ w_in, [R_QK_COLS, 2 * R_QK_COLS, 2 * R_QK_COLS + R_V_COLS], axis=-1)
    q = q.reshape(B, S, R_HEADS, R_QK_DIM)
    k = k.reshape(B, S, R_HEADS, R_QK_DIM)
    v = v.reshape(B, S, R_HEADS, R_V_DIM)
    pos = jnp.arange(S, dtype=jnp.float32)
    q = rotary(q, pos, R_ROT_BASE, R_QK_DIM)
    k = rotary(k, pos, R_ROT_BASE, R_QK_DIM) * jnp.asarray(R_QK_DIM ** -0.5, dtype=k.dtype)
    dt = q.dtype
    log_gamma = jnp.log1p(-jnp.power(2.0, -5.0 - jnp.arange(R_HEADS, dtype=jnp.float32)))
    idx = jnp.arange(CHUNK, dtype=jnp.float32)
    intra = jnp.exp(log_gamma[:, None, None] * jnp.abs(idx[:, None] - idx[None, :])).astype(dt)
    q_dec = jnp.exp(log_gamma[:, None] * (idx + 1.0)).astype(dt)[None, :, :, None]
    k_dec = jnp.exp(log_gamma[:, None] * (CHUNK - 1.0 - idx)).astype(dt)[None, :, :, None]
    chunk_dec = jnp.exp(log_gamma * CHUNK).astype(dt)[None, :, None, None]

    def to_chunks(t):
        return t.reshape(B, nc, CHUNK, R_HEADS, t.shape[-1]).transpose(1, 0, 3, 2, 4)

    def step(state, inp):
        qi, ki, vi = inp
        s = jnp.einsum('bhqd,bhkd->bhqk', qi, ki) * intra
        o = jnp.einsum('bhqk,bhkv->bhqv', s, vi) + jnp.einsum('bhqd,bhdv->bhqv', qi, state) * q_dec
        state = state * chunk_dec + jnp.einsum('bhkd,bhkv->bhdv', ki * k_dec, vi)
        return state, o

    state0 = jnp.zeros((B, R_HEADS, R_QK_DIM, R_V_DIM), dt)
    _, o = lax.scan(step, state0, (to_chunks(q), to_chunks(k), to_chunks(v)))
    o = o.transpose(1, 0, 3, 2, 4).reshape(B, S, R_HEADS, R_V_DIM)
    of = o.astype(jnp.float32)
    o = (of * lax.rsqrt(jnp.mean(of * of, axis=-1, keepdims=True) + EPS)).astype(dt)
    return (jax.nn.silu(g) * o.reshape(B, S, R_V_COLS)) @ w_o

def conv_ffn(h, w_up, conv_w, conv_b, w_down):
    u = h @ w_up
    u = lax.conv_general_dilated(u, conv_w, window_strides=(1,), padding=[(CONV_WIDTH - 1, 0)],
                                 dimension_numbers=('NWC', 'WIO', 'NWC'),
                                 feature_group_count=2 * D_FF) + conv_b
    a, b = jnp.split(u, 2, axis=-1)
    return (jax.nn.gelu(a, approximate=False) * b) @ w_down

def setup_inputs(seed: int = 0) -> dict:
    key = jax.random.key(seed)
    ks = jax.random.split(key, 14)
    f32 = jnp.float32

    def w(k, shape, fan_in):
        return jax.random.normal(k, shape, f32) * (fan_in ** -0.5)

    return {
        "x": jax.random.normal(ks[0], (BATCH, SEQ, D_MODEL), f32),
        "norm1_g": 1.0 + 0.02 * jax.random.normal(ks[1], (DEPTH, D_MODEL), f32),
        "norm2_g": 1.0 + 0.02 * jax.random.normal(ks[2], (DEPTH, D_MODEL), f32),
        "attn_w_qkv": w(ks[3], (N_A_LAYERS, D_MODEL, A_IN_COLS), D_MODEL),
        "attn_w_o": w(ks[4], (N_A_LAYERS, A_Q_COLS, D_MODEL), A_Q_COLS),
        "attn_q_gain": 1.0 + 0.02 * jax.random.normal(ks[5], (N_A_LAYERS, A_HEAD_DIM), f32),
        "attn_k_gain": 1.0 + 0.02 * jax.random.normal(ks[6], (N_A_LAYERS, A_HEAD_DIM), f32),
        "attn_sinks": 0.5 * jax.random.normal(ks[7], (N_A_LAYERS, A_HEADS), f32),
        "ret_w_in": w(ks[8], (N_B_LAYERS, D_MODEL, R_IN_COLS), D_MODEL),
        "ret_w_o": w(ks[9], (N_B_LAYERS, R_V_COLS, D_MODEL), R_V_COLS),
        "ffn_w_up": w(ks[10], (DEPTH, D_MODEL, 2 * D_FF), D_MODEL),
        "ffn_conv_w": w(ks[11], (DEPTH, CONV_WIDTH, 1, 2 * D_FF), CONV_WIDTH),
        "ffn_conv_b": 0.01 * jax.random.normal(ks[12], (DEPTH, 2 * D_FF), f32),
        "ffn_w_down": w(ks[13], (DEPTH, D_FF, D_MODEL), D_FF),
    }

def reference(x, norm1_g, norm2_g, attn_w_qkv, attn_w_o, attn_q_gain, attn_k_gain, attn_sinks,
              ret_w_in, ret_w_o, ffn_w_up, ffn_conv_w, ffn_conv_b, ffn_w_down):
    for i in range(DEPTH):
        j = i // N_MIXERS
        h = rmsnorm(x, norm1_g[i])
        if i % N_MIXERS == 0:
            x = x + swa_sink_attention(h, attn_w_qkv[j], attn_w_o[j], attn_q_gain[j], attn_k_gain[j], attn_sinks[j])
        else:
            x = x + retention(h, ret_w_in[j], ret_w_o[j])
        h = rmsnorm(x, norm2_g[i])
        x = x + conv_ffn(h, ffn_w_up[i], ffn_conv_w[i], ffn_conv_b[i], ffn_w_down[i])
    return x


_drawn_inputs = setup_inputs


def setup_inputs(seed=0):
    import zlib

    import numpy as np

    out = dict(_drawn_inputs(seed))
    spreads = {}
    factors = {'attn_q_gain': 8.0,
     'attn_k_gain': 8.0,
     'attn_sinks': 8.0,
     'ffn_conv_b': 4.667,
     'norm2_g': 2.923}
    for name, (base, spread) in spreads.items():
        noise = np.random.default_rng([zlib.crc32(name.encode()), seed]).standard_normal(out[name].shape)
        drawn = base * np.exp(spread * noise) if base else spread * noise
        out[name] = __import__('jax').numpy.asarray(drawn.astype(out[name].dtype))
    for name, factor in factors.items():
        out[name] = (out[name] * factor).astype(out[name].dtype)
    return out
```

```python
from contextlib import ExitStack

import numpy as np

import concourse.bass as bass
from concourse import mybir

F32 = mybir.dt.float32
F32R = mybir.dt.float32r
ALU = mybir.AluOpType
ACT = mybir.ActivationFunctionType
AX = mybir.AxisListType

P = 128
D = 1024
S = 512
KT = D // P
PT = S // P
EPS = 1e-6
CHUNK = 64
NCH = S // CHUNK
A_HEADS, A_DH, A_KVH = 16, 64, 2
A_ROT = A_DH // 4
A_SCALE = A_DH ** -0.5
ROPE_THETA = 500000.0
R_HEADS = 4
R_QK = D // R_HEADS
R_V = 2 * D // R_HEADS
R_BASE = 10000.0
RV_T = R_V // P
D_FF = 2816
FT = D_FF // P
KH = FT // 2
UW = 2048
DW = KH * P
KVW = 4 * 256

PAIR_KV = 0
PAIR_Q = 1
PAIR_WO = 3
PAIR_UP = (5, 40)
PAIR_DN = (5 + FT // 2, 40 + FT // 2)
PAIR_RET = PAIR_DN[0] + KT
N_PAIRS = PAIR_DN[1] + KT
assert PAIR_RET == 24 and PAIR_RET + 4 * R_HEADS == PAIR_UP[1]

NORM_A, NORM_F0, NORM_R, NORM_F1 = range(4)
SQ_BASE = (0, KT, 2 * KT, 3 * KT + R_HEADS * RV_T)
SQ_HEAD = 3 * KT
XE_WO, XE_DN0 = 0, KT
XE_RO = 2 * KT
XE_DN1 = 2 * KT + R_HEADS * KT
TD_WO, TD_UP0, TD_RO = 0, 4, 4 + FT
TD_UP1 = TD_RO + 6 * R_HEADS
ST_A, ST_F0, ST_R, ST_HEAD, ST_F1 = 0, 1, 2, 3, 3 + R_HEADS
BC_F0, BC_R, BC_HEAD, BC_F1 = 0, 1, 2, 2 + R_HEADS


def trunk(nc, xT, w_kv, w_q, w_ao, w_up0, w_dn0, w_ret, w_up1, w_dn1, gains, conv, gain_qk, sinks,
          ident_d, rot_a, rot_r, decay, out):
    ctx = ExitStack()
    with ctx:
        def sb(name, shape, dt=F32, scope=ctx):
            return scope.enter_context(nc.sbuf_tensor(name, shape, dt))

        def sem(name):
            return ctx.enter_context(nc.semaphore(name))

        x = sb("x", [P, KT, S])
        h_hi = sb("h_hi", [P, KT, S], F32R)
        h_lo = sb("h_lo", [P, KT, S], F32R)
        raw = sb("raw", [P, 2, UW])
        w_hi = sb("w_hi", [P, 2, UW], F32R)
        w_lo = sb("w_lo", [P, 2, UW], F32R)
        gain = sb("gain", [P, 4, KT])
        cvec = sb("cvec", [P, 2, FT, 8])
        ident = sb("ident", [P, P])
        ones = sb("ones", [P, 1])
        mhalf = sb("mhalf", [P, 8])
        sq = sb("sq", [P, 2, S])
        ssum = sb("ssum", [P, S])
        var = sb("var", [P, 2, PT])
        rcol = sb("rcol", [P, 2, PT])
        rbc = sb("rbc", [P, 2, S])
        ps = ctx.enter_context(nc.psum_tensor("ps", [P, 8, S], F32))

        att = ExitStack()
        qn = sb("qn", [P, PT, D], scope=att)
        kd = sb("kd", [P, PT, A_KVH, 2, A_DH], scope=att)
        va = sb("va", [P, PT, A_KVH * A_DH], scope=att)
        ve = sb("ve", [P, PT, A_KVH * A_DH], scope=att)
        qT = sb("qT", [P, NCH, KT, CHUNK], scope=att)
        kTo = sb("kTo", [P, 2, A_KVH, PT, P], scope=att)
        kTe = sb("kTe", [P, 2, A_KVH, PT, P], scope=att)
        a_hi = sb("a_hi", [P, KT, S], F32R, scope=att)
        a_lo = sb("a_lo", [P, KT, S], F32R, scope=att)
        sqq = sb("sqq", [P, 2, S], scope=att)
        qvar = sb("qvar", [P, 2, 8], scope=att)
        qss = sb("qss", [P, 2, 8], scope=att)
        qs = sb("qs", [P, 2, 8], scope=att)
        gqk = sb("gqk", [P, 2, A_DH], scope=att)
        rota = sb("rota", [P, 2, PT, A_ROT], scope=att)
        ra = sb("ra", [P, 8, A_ROT], scope=att)
        rb = sb("rb", [P, 8, A_ROT], scope=att)
        sink = sb("sink", [P, A_KVH, 4], scope=att)
        mx = sb("mx", [P, 2, 4], scope=att)
        mm = sb("mm", [P, 2, 4], scope=att)
        dm = sb("dm", [P, 2, 4], scope=att)
        es = sb("es", [P, 2, 4], scope=att)
        sm = sb("sm", [P, 2, 4], scope=att)
        rd = sb("rd", [P, 2, 4], scope=att)
        ex = qn[:, 0, :].rearrange("p (r i k) -> p r i k", r=2, i=4)
        pn = qn[:, 1, :].rearrange("p (r i k) -> p r i k", r=2, i=4)
        pT = qn[:, 2, :].rearrange("p (r f) -> p r f", r=2)
        att.close()

        ffn = ExitStack()
        g_hi = sb("g_hi", [P, FT, S], F32R, scope=ffn)
        g_lo = sb("g_lo", [P, FT, S], F32R, scope=ffn)
        u = sb("u", [P, 2, S + 2], scope=ffn)
        y = sb("y", [P, 2, S], scope=ffn)
        gp = sb("gp", [P, S], scope=ffn)
        ffn.close()

        ret = ExitStack()
        qk = sb("qk", [P, 4, S], scope=ret)
        rt = sb("rt", [P, 4, S], scope=ret)
        vr = sb("vr", [P, PT, R_V], scope=ret)
        pr = sb("pr", [P, PT, S], scope=ret)
        sg = sb("sg", [P, RV_T, S], scope=ret)
        o_hi = sb("o_hi", [P, RV_T, S], F32R, scope=ret)
        o_lo = sb("o_lo", [P, RV_T, S], F32R, scope=ret)
        yf = sb("yf", [P, RV_T, S], scope=ret)
        tab = sb("tab", [P, 2, S], scope=ret)
        dec = sb("dec", [P, R_HEADS, S], scope=ret)
        csr = sb("csr", [P, 2, S], scope=ret)
        ret.close()

        x_in = [sem(f"x_in{k}") for k in range(KT)]
        c_in = sem("c_in")
        r_in = sem("r_in")
        o_out = sem("o_out")
        cst = sem("cst")
        w_loaded = [sem("w_loaded0"), sem("w_loaded1")]
        w_hi_ok, w_lo_ok, w_used = sem("w_hi_ok"), sem("w_lo_ok"), sem("w_used")
        tile_done = sem("tile_done")
        h_hi_ok, h_ready = sem("h_hi_ok"), sem("h_ready")
        sq_ok, ssum_ok = sem("sq_ok"), sem("ssum_ok")
        col_done, var_ok, r_ok, bc_done, bc_ok = (sem(n) for n in ("col_done", "var_ok", "r_ok", "bc_done", "bc_ok"))
        xe_ok = sem("xe_ok")
        v_ok, ve_ok = sem("v_ok"), sem("ve_ok")
        qsq_ok, qss_ok, qvar_ok, qs_ok, qn_ok, qrot_ok = (sem(n) for n in (
            "qsq_ok", "qss_ok", "qvar_ok", "qs_ok", "qn_ok", "qrot_ok"))
        pool_step = sem("pool_step")
        tp_done, tp_ok = sem("tp_done"), sem("tp_ok")
        s_done, mx_ok, m_ok, e_ok, ex_ok, sum_ok, den_ok, rd_ok, pn_ok = (sem(n) for n in (
            "s_done", "mx_ok", "m_ok", "e_ok", "ex_ok", "sum_ok", "den_ok", "rd_ok", "pn_ok"))
        pz_ok = sem("pz_ok")
        pt_done, pt_ok, pv_done, ahi_ok, alo_ok = (sem(n) for n in (
            "pt_done", "pt_ok", "pv_done", "ahi_ok", "alo_ok"))
        u_ok, yb_ok, y1_ok, y_ok, ge_ok, gp_ok, ghi_ok, glo_ok = (sem(n) for n in (
            "u_ok", "yb_ok", "y1_ok", "y_ok", "ge_ok", "gp_ok", "ghi_ok", "glo_ok"))
        csr_ok, rt_ok, qk_ok, vr_ok, rs_done, pr_ok, gx_ok, sg_ok = (sem(n) for n in (
            "csr_ok", "rt_ok", "qk_ok", "vr_ok", "rs_done", "pr_ok", "gx_ok", "sg_ok"))
        o_done, ot_ok, yf_ok, ohi_ok, olo_ok = (sem(n) for n in ("o_done", "ot_ok", "yf_ok", "ohi_ok", "olo_ok"))

        block = ctx.enter_context(nc.Block())

        def bank_of(n):
            return (n % PT) + (4 if 4 <= n < 8 else 0)

        GROUPS = [(g // NCH, g % NCH) for g in range(A_KVH * NCH)]

        @block.sync
        def _(sp):
            def load(src, pair, s, cols, first=False):
                if not first:
                    sp.wait_ge(w_lo_ok, 2 * pair + s - 1)
                sp.dma_start(raw[:, s, 0:cols], src).then_inc(w_loaded[s], 16)

            for k in range(KT):
                sp.dma_start(x[:, k, :], xT[k]).then_inc(x_in[k], 16)
                if k == 3:
                    load(w_kv[0], PAIR_KV, 0, KVW, first=True)
            load(w_kv[1], PAIR_KV, 1, KVW, first=True)
            for cb in range(2):
                for s in range(2):
                    load(w_q[2 * cb + s], PAIR_Q + cb, s, UW)
            for j in range(2):
                for s in range(2):
                    load(w_ao[2 * j + s], PAIR_WO + j, s, UW)

            def rows(src, i):
                return src[bass.ds(i, 1), :, :].rearrange("o p f -> (o p) f")

            def mlp(layer, w_up, w_dn):
                with sp.Fori(0, FT // 2) as j:
                    for s in range(2):
                        load(rows(w_up, 2 * j + s), PAIR_UP[layer] + j, s, UW)
                with sp.Fori(0, KT) as j:
                    for s in range(2):
                        load(rows(w_dn, 2 * j + s), PAIR_DN[layer] + j, s, DW)

            mlp(0, w_up0, w_dn0)
            with sp.Fori(0, 4 * R_HEADS) as j:
                for s in range(2):
                    load(rows(w_ret, 2 * j + s), PAIR_RET + j, s, UW)
            mlp(1, w_up1, w_dn1)
            for m in range(KT):
                sp.wait_ge(xe_ok, XE_DN1 + m + 1)
                sp.dma_start(out[m], x[:, m, :]).then_inc(o_out, 16)
            sp.wait_ge(o_out, 16 * KT)

        @block.scalar
        def _(act):
            for dst, src in ((gain[:, :, :], gains), (cvec[:, :, :, :], conv), (gqk[:, :, :], gain_qk),
                             (sink[:, :, :], sinks), (ident[:, :], ident_d), (rota[:, :, :, :], rot_a)):
                act.dma_start(dst, src).then_inc(c_in, 16)


            def split(pair, s, cols, first=False):
                act.wait_ge(w_loaded[s], 16 * (pair + 1))
                if not first:
                    act.wait_ge(w_used, 2 * pair + s - 1)
                nc.scalar.activation(w_hi[:, s, 0:cols], raw[:, s, 0:cols], ACT.Copy).then_inc(w_hi_ok, 1)

            def hi_tile(norm, m):
                nc.scalar.activation(h_hi[:, m, :], x[:, m, :], ACT.Copy,
                                     scale=gain[:, norm, m:m + 1]).then_inc(h_hi_ok, 1)
                square(SQ_BASE[norm], m, x[:, m, :])

            def square(base, m, src):
                n = base + m
                if not (isinstance(n, int) and n < 2):
                    act.wait_ge(ssum_ok, n - 1)
                nc.scalar.activation(sq[:, m % 2, :], src, ACT.Square).then_inc(sq_ok, 1)

            def broadcast_out(n, which):
                act.wait_ge(bc_done, n + 1)
                nc.scalar.activation(rbc[:, which, :], ps[:, 7, :], ACT.Copy).then_inc(bc_ok, 1)

            act.wait_ge(c_in, 16 * 6)
            for k in range(KT):
                act.wait_ge(x_in[k], 16)
                hi_tile(NORM_A, k)
                if k == 3:
                    split(PAIR_KV, 0, KVW, first=True)
            split(PAIR_KV, 1, KVW, first=True)
            split(PAIR_Q, 0, UW)

            def q_squares(items, width, col0):
                for n in items:
                    t = n % PT
                    if n >= 2:
                        act.wait_ge(qss_ok, n - 1)
                    nc.scalar.activation(sqq[:, n % 2, 0:width], ps[:, bank_of(n), col0:col0 + width], ACT.Square,
                                         scale=rcol[:, 0, t:t + 1]).then_inc(qsq_ok, 1)

            act.wait_ge(w_used, 2)
            act.wait_ge(r_ok, ST_A + 1)
            for t in range(PT):
                nc.scalar.activation(va[:, t, :], ps[:, t, P:2 * P], ACT.Copy,
                                     scale=rcol[:, 0, t:t + 1]).then_inc(v_ok, 1)
            q_squares(range(0, 4), P, 0)
            split(PAIR_Q, 1, UW)
            split(PAIR_Q + 1, 0, UW)
            act.wait_ge(w_used, 4)
            q_squares(range(4, 8), S, 0)
            split(PAIR_Q + 1, 1, UW)
            split(PAIR_WO, 0, UW)
            act.wait_ge(w_used, 6)
            q_squares(range(8, 12), S, 0)
            split(PAIR_WO, 1, UW)

            for g in range(10):
                act.wait_ge(tp_done, g + 1)
                b = ps[:, 4 + g % 4, :]
                if g < 2:
                    own = b.rearrange("p (t c) -> p t c", c=P)
                    for par in range(2):
                        rows = slice(par * A_DH, (par + 1) * A_DH)
                        nc.scalar.activation(kTo[rows, par, g, :, :], own[rows], ACT.Copy)
                        nc.scalar.activation(kTe[rows, par, g, :, 0:CHUNK], own[rows, :, 0:CHUNK], ACT.Copy)
                        last = nc.scalar.activation(kTe[rows, par, g, 1:PT, CHUNK:P], own[rows, 0:PT - 1, CHUNK:P],
                                                    ACT.Copy)
                    last.then_inc(tp_ok, 1)
                else:
                    nc.scalar.activation(qT[:, :, g - 2, :], b.rearrange("p (n c) -> p n c", c=CHUNK),
                                         ACT.Copy).then_inc(tp_ok, 1)

            def exps(g):
                _, n = GROUPS[g]
                nk = CHUNK if n == 0 else P
                act.wait_ge(e_ok, g + 1)
                nc.scalar.activation(ex[:, g % 2, :, 0:nk], ex[:, g % 2, :, 0:nk], ACT.Exp)
                nc.scalar.activation(es[:, g % 2, :], dm[:, g % 2, :], ACT.Exp).then_inc(ex_ok, 1)

            def probs_out(g):
                act.wait_ge(pt_done, g + 1)
                nc.scalar.activation(pT[:, g % 2, :], ps[:, 2 + g % 2, :], ACT.Copy).then_inc(pt_ok, 1)

            def heads_out(g):
                c, n = GROUPS[g]
                act.wait_ge(pv_done, g + 1)
                nc.scalar.activation(a_hi[:, 4 * c:4 * c + 4, n * CHUNK:(n + 1) * CHUNK],
                                     ps[:, 4 + g % 2, 0:4 * CHUNK].rearrange("p (j q) -> p j q", q=CHUNK),
                                     ACT.Copy).then_inc(ahi_ok, 1)

            NG = len(GROUPS)
            for st in range(NG + 3):
                if st < NG:
                    exps(st)
                if 1 <= st < NG + 1:
                    probs_out(st - 1)
                if 2 <= st < NG + 2:
                    heads_out(st - 2)

            for j in range(2):
                for s in range(2):
                    for e in range(2):
                        m = 4 * j + 2 * s + e
                        act.wait_ge(xe_ok, XE_WO + m + 1)
                        hi_tile(NORM_F0, m)
                        if e == 0:
                            split(PAIR_WO + j + 1, s, UW)

            def mlp(layer, last_layer):
                up, dn = PAIR_UP[layer], PAIR_DN[layer]

                def up_pair(j, s, cols, first=False):
                    i = 2 * j + s
                    f = FT * layer + i
                    if first and s == 0:
                        broadcast_out(BC_F1 if layer else BC_F0, 0)
                    for ab in range(2):
                        act.wait_ge(u_ok, 2 * f + ab + 1)
                        c = cvec[:, layer, bass.ds(i, 1), 4 * ab + 2:4 * ab + 4].rearrange("p o f -> p (o f)")
                        nc.scalar.activation(y[:, ab, :], u[:, ab, 2:S + 2], ACT.Identity,
                                             scale=c[:, 0:1], bias=c[:, 1:2]).then_inc(yb_ok, 1)
                    split(up + j + 1, s, cols)
                    act.wait_ge(y_ok, 2 * f + 1)
                    nc.scalar.activation(y[:, 0, :], y[:, 0, :], ACT.Gelu).then_inc(ge_ok, 1)
                    act.wait_ge(gp_ok, f + 1)
                    nc.scalar.activation(g_hi[:, bass.ds(i, 1), :].rearrange("p o f -> p (o f)"), gp[:, :],
                                         ACT.Copy).then_inc(ghi_ok, 1)

                for s in range(2):
                    up_pair(0, s, UW, first=True)
                with act.Fori(1, FT // 2 - 1) as j:
                    for s in range(2):
                        up_pair(j, s, UW)
                for s in range(2):
                    up_pair(FT // 2 - 1, s, DW)

                def down(m, e, cols):
                    for s in range(2):
                        if cols:
                            split(dn + m + 1, s, cols)
                    if not last_layer:
                        act.wait_ge(ssum_ok, SQ_BASE[NORM_R] + m - 1)
                        act.wait_ge(xe_ok, XE_DN0 + m + 1)
                        gv = gain[:, NORM_R, bass.ds(m, 1)]
                        nc.scalar.activation(h_hi[:, bass.ds(m, 1), :].rearrange("p o f -> p (o f)"),
                                             x[:, bass.ds(m, 1), :].rearrange("p o f -> p (o f)"), ACT.Copy,
                                             scale=gv).then_inc(h_hi_ok, 1)
                        nc.scalar.activation(sq[:, e, :], x[:, bass.ds(m, 1), :].rearrange("p o f -> p (o f)"),
                                             ACT.Square).then_inc(sq_ok, 1)

                with act.Fori(0, KT // 2 - 1) as j:
                    for e in range(2):
                        down(2 * j + e, e, DW)
                down(KT - 2, 0, DW)
                down(KT - 1, 1, 0 if last_layer else UW)

            mlp(0, False)

            def qkvg(h, first):
                p0 = PAIR_RET if first else PAIR_RET + 4 * h - 1
                nxt = p0 + 1
                split(nxt, 0, UW)
                if not first:
                    broadcast_out(BC_HEAD + h - 1, 1)
                    for m in range(RV_T):
                        head_hi(h - 1, m)
                split(nxt, 1, UW)
                if not first:
                    for s in range(2):
                        split(p0 + 2, s, UW)
                pv = PAIR_RET + 1 if first else p0 + 2
                split(pv + 1, 0, UW)
                act.wait_ge(w_used, 2 * pv + 2)
                for t in range(PT):
                    nc.scalar.activation(vr[:, t, :], ps[:, 4 + t, :], ACT.Copy,
                                         scale=rcol[:, 0, t:t + 1]).then_inc(vr_ok, 1)
                split(pv + 1, 1, UW)
                for s in range(2):
                    for e in range(2):
                        m = 2 * s + e
                        act.wait_ge(gx_ok, 4 * h + m + 1)
                        nc.scalar.activation(sg[:, m, :], sg[:, m, :], ACT.Silu).then_inc(sg_ok, 1)
                    split(pv + 2, s, UW)
                for m in range(RV_T):
                    act.wait_ge(o_done, 4 * h + m + 1)
                    square(SQ_HEAD + 4 * h, m, ps[:, m, :])

            def head_hi(h, m):
                act.wait_ge(yf_ok, 4 * h + m + 1)
                nc.scalar.activation(o_hi[:, m, :], yf[:, m, :], ACT.Copy).then_inc(ohi_ok, 1)

            act.wait_ge(w_used, 2 * PAIR_RET)
            act.dma_start(tab[:, :, :], rot_r).then_inc(r_in, 16)
            act.dma_start(dec[:, :, :], decay).then_inc(r_in, 16)
            broadcast_out(BC_R, 0)
            qkvg(0, True)
            with act.Fori(1, R_HEADS) as h:
                qkvg(h, False)
            broadcast_out(BC_HEAD + R_HEADS - 1, 1)
            for m in range(RV_T):
                head_hi(R_HEADS - 1, m)
            for s in range(2):
                split(PAIR_UP[1], s, UW)
                for e in range(4):
                    m = 4 * s + e
                    act.wait_ge(xe_ok, XE_RO + KT * (R_HEADS - 1) + m + 1)
                    hi_tile(NORM_F1, m)

            mlp(1, True)

        @block.vector
        def _(dve):
            def split(pair, s, cols):
                dve.wait_ge(w_hi_ok, 2 * pair + s + 1)
                nc.vector.tensor_tensor(w_lo[:, s, 0:cols], raw[:, s, 0:cols], w_hi[:, s, 0:cols].bitcast(F32),
                                        ALU.subtract).then_inc(w_lo_ok, 1)

            def lo_tile(norm, m, xm, hm, lm, g):
                dve.wait_ge(h_hi_ok, KT * norm + m + 1)
                nc.vector.scalar_tensor_tensor(lm, xm, g, hm.bitcast(F32), ALU.mult,
                                               ALU.subtract).then_inc(h_ready, 1)

            def lo_static(norm, m):
                lo_tile(norm, m, x[:, m, :], h_hi[:, m, :], h_lo[:, m, :], gain[:, norm, m:m + 1])

            def variance(n, which, width):
                dve.wait_ge(col_done, n + 1)
                nc.vector.tensor_scalar(var[:, which, :], ps[:, 6, 0:PT], 1.0 / width, EPS, ALU.mult,
                                        ALU.add).then_inc(var_ok, 1)

            def add_tile(m, bank):
                nc.vector.tensor_tensor(x[:, m, :], ps[:, bank, :], x[:, m, :], ALU.add).then_inc(xe_ok, 1)

            dve.wait_ge(c_in, 16 * 6)
            for k in range(KT):
                lo_static(NORM_A, k)
                if k == 3:
                    split(PAIR_KV, 0, KVW)
            split(PAIR_KV, 1, KVW)
            variance(ST_A, 0, D)
            split(PAIR_Q, 0, UW)

            def q_var(n, heads):
                dve.wait_ge(qsq_ok, n + 1)
                nc.vector.tensor_reduce(qss[:, n % 2, 0:heads],
                                        sqq[:, n % 2, 0:heads * A_DH].rearrange("p (h d) -> p h d", d=A_DH),
                                        AX.X, ALU.add).then_inc(qss_ok, 1)
                dve.wait_ge(qss_ok, n + 1)
                nc.vector.tensor_scalar(qvar[:, n % 2, 0:heads], qss[:, n % 2, 0:heads], 1.0 / A_DH, EPS,
                                        ALU.mult, ALU.add).then_inc(qvar_ok, 1)

            def q_norm(n, heads):
                t = n % PT
                src = ps[:, bank_of(n), 0:heads * A_DH].rearrange("p (h d) -> p h d", d=A_DH)
                if n < 4:
                    dst = kd[:, t, :, 0, :]
                else:
                    cb = (n - 4) // 4
                    dst = qn[:, t, cb * S:(cb + 1) * S].rearrange("p (h d) -> p h d", d=A_DH)
                dve.wait_ge(qs_ok, n + 1)
                nc.vector.scalar_tensor_tensor(dst, src, rcol[:, 0, t:t + 1],
                                               qs[:, n % 2, 0:heads].unsqueeze(2).to_broadcast([P, heads, A_DH]),
                                               ALU.mult, ALU.mult).then_inc(qn_ok, 1)

            def q_items(items, heads):
                for n in items:
                    q_var(n, heads)
                    if n > items[0]:
                        q_norm(n - 1, heads)
                q_norm(items[-1], heads)

            q_items(range(0, 4), 2)
            split(PAIR_Q, 1, UW)
            split(PAIR_Q + 1, 0, UW)
            q_items(range(4, 8), 8)
            split(PAIR_Q + 1, 1, UW)
            split(PAIR_WO, 0, UW)
            q_items(range(8, 12), 8)
            split(PAIR_WO, 1, UW)

            def softmax_top(g):
                c, n = GROUPS[g]
                nk = CHUNK if n == 0 else P
                r = g % 2
                sc = ps[:, r, :].rearrange("p (i k) -> p i k", k=P)[:, :, 0:nk]
                dve.wait_ge(s_done, g + 1)
                nc.vector.tensor_reduce(mx[:, r, :], sc, AX.X, ALU.max).then_inc(mx_ok, 1)
                dve.wait_ge(mx_ok, g + 1)
                nc.vector.scalar_tensor_tensor(mm[:, r, :], mx[:, r, :], A_SCALE, sink[:, c, :], ALU.mult,
                                               ALU.max).then_inc(m_ok, 1)
                dve.wait_ge(m_ok, g + 1)
                nc.vector.tensor_tensor(dm[:, r, :], sink[:, c, :], mm[:, r, :], ALU.subtract)
                if g >= 2:
                    dve.wait_ge(pn_ok, g - 1)
                nc.vector.scalar_tensor_tensor(ex[:, r, :, 0:nk], sc, A_SCALE,
                                               mm[:, r, :].unsqueeze(2).to_broadcast([P, 4, nk]), ALU.mult,
                                               ALU.subtract).then_inc(e_ok, 1)

            def softmax_bottom(g):
                _, n = GROUPS[g]
                nk = CHUNK if n == 0 else P
                r = g % 2
                dve.wait_ge(ex_ok, g + 1)
                nc.vector.tensor_reduce(sm[:, r, :], ex[:, r, :, 0:nk], AX.X, ALU.add).then_inc(sum_ok, 1)
                dve.wait_ge(sum_ok, g + 1)
                nc.vector.tensor_tensor(sm[:, r, :], sm[:, r, :], es[:, r, :], ALU.add).then_inc(den_ok, 1)
                dve.wait_ge(den_ok, g + 1)
                nc.vector.reciprocal(rd[:, r, :], sm[:, r, :]).then_inc(rd_ok, 1)

            def heads_lo(g):
                c, n = GROUPS[g]
                dst = (slice(None), slice(4 * c, 4 * c + 4), slice(n * CHUNK, (n + 1) * CHUNK))
                dve.wait_ge(ahi_ok, g + 1)
                nc.vector.tensor_tensor(a_lo[dst], ps[:, 4 + g % 2, 0:4 * CHUNK].rearrange("p (j q) -> p j q", q=CHUNK),
                                        a_hi[dst].bitcast(F32), ALU.subtract).then_inc(alo_ok, 1)

            NG = len(GROUPS)
            softmax_top(0)
            for st in range(NG + 3):
                if st + 1 < NG:
                    softmax_top(st + 1)
                if st < NG:
                    softmax_bottom(st)
                if 2 <= st < NG + 2:
                    heads_lo(st - 2)

            for j in range(2):
                for s in range(2):
                    for e in range(2):
                        m = 4 * j + 2 * s + e
                        if e == 0:
                            dve.wait_ge(tile_done, TD_WO + 2 * j + s + 1)
                        else:
                            dve.wait_ge(w_used, 2 * (PAIR_WO + j) + s + 1)
                        add_tile(m, m % 4)
                        if m > 0:
                            lo_static(NORM_F0, m - 1)
                        if e == 1:
                            split(PAIR_WO + j + 1, s, UW)
            lo_static(NORM_F0, KT - 1)

            def mlp(layer, last_layer):
                up, dn = PAIR_UP[layer], PAIR_DN[layer]
                td = (TD_UP0, TD_UP1)[layer]

                def up_pair(j, s, cols, first=False):
                    i = 2 * j + s
                    f = FT * layer + i
                    c = cvec[:, layer, bass.ds(i, 1), :].rearrange("p o f -> p (o f)")
                    if first and s == 0:
                        variance(ST_F1 if layer else ST_F0, 0, D)
                        dve.wait_ge(cst, 9 + layer)
                        dve.wait_ge(bc_ok, (BC_F1 if layer else BC_F0) + 1)
                    dve.wait_ge(tile_done, td + i + 1)
                    nc.vector.tensor_tensor(u[:, 0, 2:S + 2], ps[:, 2 * s, :], rbc[:, 0, :], ALU.mult).then_inc(u_ok, 1)
                    dve.wait_ge(w_used, 2 * (up + j) + s + 1)
                    nc.vector.tensor_tensor(u[:, 1, 2:S + 2], ps[:, 2 * s + 1, :], rbc[:, 0, :],
                                            ALU.mult).then_inc(u_ok, 1)
                    for ab in range(2):
                        dve.wait_ge(yb_ok, 2 * f + ab + 1)
                        nc.vector.scalar_tensor_tensor(y[:, ab, :], u[:, ab, 1:S + 1], c[:, 4 * ab + 1:4 * ab + 2],
                                                       y[:, ab, :], ALU.mult, ALU.add).then_inc(y1_ok, 1)
                    for ab in range(2):
                        dve.wait_ge(y1_ok, 2 * f + ab + 1)
                        nc.vector.scalar_tensor_tensor(y[:, ab, :], u[:, ab, 0:S], c[:, 4 * ab:4 * ab + 1],
                                                       y[:, ab, :], ALU.mult, ALU.add).then_inc(y_ok, 1)
                    split(up + j + 1, s, cols)
                    dve.wait_ge(ge_ok, f + 1)
                    dve.wait_ge(y_ok, 2 * f + 2)
                    nc.vector.tensor_tensor(gp[:, :], y[:, 0, :], y[:, 1, :], ALU.mult).then_inc(gp_ok, 1)
                    dve.wait_ge(ghi_ok, f + 1)
                    gi = (slice(None), bass.ds(i, 1), slice(None))
                    nc.vector.tensor_tensor(g_lo[gi].rearrange("p o f -> p (o f)"), gp[:, :],
                                            g_hi[gi].rearrange("p o f -> p (o f)").bitcast(F32),
                                            ALU.subtract).then_inc(glo_ok, 1)

                for s in range(2):
                    up_pair(0, s, UW, first=True)
                with dve.Fori(1, FT // 2 - 1) as j:
                    for s in range(2):
                        up_pair(j, s, UW)
                for s in range(2):
                    up_pair(FT // 2 - 1, s, DW)

                def down(m, e, cols):
                    if cols:
                        split(dn + m + 1, 0, cols)
                    dve.wait_ge(w_used, 2 * (dn + m) + 2)
                    xm = x[:, bass.ds(m, 1), :].rearrange("p o f -> p (o f)")
                    nc.vector.tensor_tensor(xm, ps[:, 4 + e, :], xm, ALU.add).then_inc(xe_ok, 1)
                    if cols:
                        split(dn + m + 1, 1, cols)
                    if not last_layer:
                        lo_tile(NORM_R, m, xm, h_hi[:, bass.ds(m, 1), :].rearrange("p o f -> p (o f)"),
                                h_lo[:, bass.ds(m, 1), :].rearrange("p o f -> p (o f)"),
                                gain[:, NORM_R, bass.ds(m, 1)])

                with dve.Fori(0, KT // 2 - 1) as j:
                    for e in range(2):
                        down(2 * j + e, e, DW)
                down(KT - 2, 0, DW)
                down(KT - 1, 1, 0 if last_layer else UW)

            mlp(0, False)

            def rotary(p, s, h, first=False):
                dve.wait_ge(w_used, 2 * p + s + 1)
                if first:
                    dve.wait_ge(csr_ok, 2)
                else:
                    dve.wait_ge(qk_ok, 4 * h + 2 * s)
                a, b = ps[:, 2 * s, :], ps[:, 2 * s + 1, :]
                nc.vector.tensor_tensor(rt[:, 0, :], a, csr[:, 0, :], ALU.mult)
                nc.vector.tensor_tensor(rt[:, 1, :], b, csr[:, 1, :], ALU.mult).then_inc(rt_ok, 1)
                nc.vector.tensor_tensor(rt[:, 2, :], b, csr[:, 0, :], ALU.mult)
                nc.vector.tensor_tensor(rt[:, 3, :], a, csr[:, 1, :], ALU.mult).then_inc(rt_ok, 1)

            def qkvg(h, first):
                p0 = PAIR_RET if first else PAIR_RET + 4 * h - 1
                rotary(p0, 0, h, first)
                split(p0 + 1, 0, UW)
                if not first:
                    for m in range(RV_T):
                        head_lo(h - 1, m)
                rotary(p0, 1, h)
                split(p0 + 1, 1, UW)
                if not first:
                    for s in range(2):
                        project(h - 1, s, p0 + 1)
                        split(p0 + 2, s, UW)
                pv = PAIR_RET + 1 if first else p0 + 2
                split(pv + 1, 0, UW)
                split(pv + 1, 1, UW)
                for t in range(PT):
                    dve.wait_ge(rs_done, 4 * h + t + 1)
                    nc.vector.tensor_tensor(pr[:, t, 0:S - t * P], ps[:, t, 0:S - t * P],
                                            dec[:, bass.ds(h, 1), 0:S - t * P].rearrange("p o f -> p (o f)"),
                                            ALU.mult).then_inc(pr_ok, 1)
                for s in range(2):
                    dve.wait_ge(w_used, 2 * (pv + 1) + s + 1)
                    for e in range(2):
                        m = 2 * s + e
                        nc.vector.tensor_tensor(sg[:, m, :], ps[:, 4 + m, :], rbc[:, 0, :],
                                                ALU.mult).then_inc(gx_ok, 1)
                    split(pv + 2, s, UW)
                for m in range(RV_T):
                    dve.wait_ge(sq_ok, SQ_HEAD + 4 * h + m + 1)
                    dve.wait_ge(sg_ok, 4 * h + m + 1)
                    nc.vector.tensor_tensor(sg[:, m, :], ps[:, m, :], sg[:, m, :], ALU.mult).then_inc(ot_ok, 1)
                variance(ST_HEAD + h, 1, R_V)

            def head_lo(h, m):
                dve.wait_ge(ohi_ok, 4 * h + m + 1)
                nc.vector.tensor_tensor(o_lo[:, m, :], yf[:, m, :], o_hi[:, m, :].bitcast(F32),
                                        ALU.subtract).then_inc(olo_ok, 1)

            def project(h, s, p):
                for e in range(4):
                    if e < 3:
                        dve.wait_ge(tile_done, TD_RO + 6 * h + 3 * s + e + 1)
                    else:
                        dve.wait_ge(w_used, 2 * p + s + 1)
                    add_tile(4 * s + e, 4 + e)

            dve.wait_ge(r_in, 32)
            variance(ST_R, 0, D)
            qkvg(0, True)
            with dve.Fori(1, R_HEADS) as h:
                qkvg(h, False)
            for m in range(RV_T):
                head_lo(R_HEADS - 1, m)
            for s in range(2):
                project(R_HEADS - 1, s, PAIR_UP[1] - 1)
                split(PAIR_UP[1], s, UW)
                for e in range(4):
                    lo_static(NORM_F1, 4 * s + e)

            mlp(1, True)

        @block.gpsimd
        def _(pool):
            steps = [0]

            def step(ins):
                steps[0] += 1
                ins.then_inc(pool_step, 1)
                pool.wait_ge(pool_step, steps[0])

            nc.gpsimd.memset(ones[:, :], 1.0).then_inc(cst, 1)
            nc.gpsimd.memset(mhalf[:, :], -0.5).then_inc(cst, 1)
            pool.wait_ge(cst, 2)
            nc.gpsimd.memset(kTo[A_DH:P, 0, :, :, :], 0.0).then_inc(cst, 1)
            nc.gpsimd.memset(kTe[A_DH:P, 0, :, :, :], 0.0).then_inc(cst, 1)
            nc.gpsimd.memset(ve[CHUNK:P, 0, :], 0.0).then_inc(cst, 1)
            pool.wait_ge(cst, 5)
            nc.gpsimd.memset(kTo[0:A_DH, 1, :, :, :], 0.0).then_inc(cst, 1)
            nc.gpsimd.memset(kTe[0:A_DH, 1, :, :, :], 0.0).then_inc(cst, 1)
            pool.wait_ge(cst, 7)
            nc.gpsimd.memset(kTe[:, :, :, 0, CHUNK:P], 0.0).then_inc(cst, 1)
            pool.wait_ge(cst, 8)

            def add_squares(base, tiles):
                for m in range(1, tiles):
                    pool.wait_ge(sq_ok, base + m + 1)
                    if m == 1:
                        nc.gpsimd.tensor_tensor(ssum[:, :], sq[:, 0, :], sq[:, 1, :], ALU.add).then_inc(ssum_ok, 2)
                    else:
                        pool.wait_ge(ssum_ok, base + m)
                        nc.gpsimd.tensor_tensor(ssum[:, :], ssum[:, :], sq[:, m % 2, :], ALU.add).then_inc(ssum_ok, 1)

            def inv_root(n, which):
                pool.wait_ge(var_ok, n + 1)
                nc.gpsimd.tensor_tensor(rcol[:, which, :], var[:, which, :], mhalf[:, 0:PT],
                                        ALU.pow).then_inc(r_ok, 1)

            add_squares(SQ_BASE[NORM_A], KT)
            inv_root(ST_A, 0)
            pool.wait_ge(c_in, 16 * 6)

            def q_root(n, heads):
                pool.wait_ge(qvar_ok, n + 1)
                nc.gpsimd.tensor_tensor(qs[:, n % 2, 0:heads], qvar[:, n % 2, 0:heads], mhalf[:, 0:heads],
                                        ALU.pow).then_inc(qs_ok, 1)

            def q_rotate(n, heads):
                t = n % PT
                v = kd[:, t, :, 0, :] if n < 4 else \
                    qn[:, t, (n - 4) // 4 * S:((n - 4) // 4 + 1) * S].rearrange("p (h d) -> p h d", d=A_DH)
                gi = 1 if n < 4 else 0
                half = A_ROT // 2
                pool.wait_ge(qn_ok, n + 1)
                step(nc.gpsimd.tensor_tensor(v, v, gqk[:, gi, :].unsqueeze(1).to_broadcast([P, heads, A_DH]), ALU.mult))
                nc.gpsimd.tensor_tensor(ra[:, 0:heads, :], v[:, :, 0:A_ROT],
                                        rota[:, 0, t, :].unsqueeze(1).to_broadcast([P, heads, A_ROT]), ALU.mult)
                nc.gpsimd.tensor_tensor(rb[:, 0:heads, 0:half], v[:, :, half:A_ROT],
                                        rota[:, 1, t, 0:half].unsqueeze(1).to_broadcast([P, heads, half]), ALU.mult)
                step(nc.gpsimd.tensor_tensor(rb[:, 0:heads, half:A_ROT], v[:, :, 0:half],
                                             rota[:, 1, t, half:A_ROT].unsqueeze(1).to_broadcast([P, heads, half]),
                                             ALU.mult))
                last = nc.gpsimd.tensor_tensor(v[:, :, 0:A_ROT], ra[:, 0:heads, :], rb[:, 0:heads, :], ALU.add)
                if n < 4:
                    step(last)
                    last = nc.gpsimd.tensor_copy(kd[:, t, :, 1, :], kd[:, t, :, 0, :])
                last.then_inc(qrot_ok, 1)

            def q_items(items, heads):
                for n in items:
                    q_root(n, heads)
                    if n > items[0]:
                        q_rotate(n - 1, heads)
                q_rotate(items[-1], heads)

            q_items(range(0, 4), 2)
            pool.wait_ge(v_ok, 4)
            pool.wait_ge(qrot_ok, 4)
            nc.gpsimd.tensor_copy(ve[0:CHUNK, :, :], va[0:CHUNK, :, :]).then_inc(ve_ok, 1)
            pool.wait_ge(ve_ok, 1)
            nc.gpsimd.tensor_copy(ve[CHUNK:P, 1:PT, :], va[CHUNK:P, 0:PT - 1, :]).then_inc(ve_ok, 1)
            pool.wait_ge(ve_ok, 2)
            q_items(range(4, 8), 8)
            q_items(range(8, 12), 8)

            for g, (c, n) in enumerate(GROUPS):
                r = g % 2
                nk = CHUNK if n == 0 else P
                if g >= 2:
                    pool.wait_ge(pt_done, g - 1)
                if g == 0:
                    pool.wait_ge(s_done, 1)
                if n == 0:
                    nc.gpsimd.memset(pn[:, r, :, CHUNK:P], 0.0).then_inc(pz_ok, 1)
                    pool.wait_ge(pz_ok, c + 1)
                pool.wait_ge(rd_ok, g + 1)
                nc.gpsimd.tensor_tensor(pn[:, r, :, 0:nk], ex[:, r, :, 0:nk],
                                        rd[:, r, :].unsqueeze(2).to_broadcast([P, 4, nk]), ALU.mult).then_inc(pn_ok, 1)

            add_squares(SQ_BASE[NORM_F0], KT)
            pool.wait_ge(w_used, 2 * PAIR_UP[0])
            nc.gpsimd.memset(u[:, :, 0:2], 0.0).then_inc(cst, 1)
            inv_root(ST_F0, 0)
            add_squares(SQ_BASE[NORM_R], KT)
            inv_root(ST_R, 0)

            pool.wait_ge(r_in, 32)
            pool.wait_ge(bc_ok, BC_R + 1)
            for i in range(2):
                nc.gpsimd.tensor_tensor(csr[:, i, :], tab[:, i, :], rbc[:, 0, :], ALU.mult).then_inc(csr_ok, 1)

            def qkvg(h, first):
                for s in range(2):
                    for i, op in ((0, ALU.subtract), (1, ALU.add)):
                        pool.wait_ge(rt_ok, 4 * h + 2 * s + i + 1)
                        nc.gpsimd.tensor_tensor(qk[:, 2 * s + i, :], rt[:, 2 * i, :], rt[:, 2 * i + 1, :],
                                                op).then_inc(qk_ok, 1)
                    if s == 0 and not first:
                        head_out(h - 1)
                add_squares(SQ_HEAD + 4 * h, RV_T)
                inv_root(ST_HEAD + h, 1)

            def head_out(h):
                pool.wait_ge(bc_ok, BC_HEAD + h + 1)
                for m in range(RV_T):
                    nc.gpsimd.tensor_tensor(yf[:, m, :], sg[:, m, :], rbc[:, 1, :], ALU.mult).then_inc(yf_ok, 1)

            qkvg(0, True)
            with pool.Fori(1, R_HEADS) as h:
                qkvg(h, False)
            head_out(R_HEADS - 1)
            add_squares(SQ_BASE[NORM_F1], KT)
            pool.wait_ge(w_used, 2 * PAIR_UP[1])
            nc.gpsimd.memset(u[:, :, 0:2], 0.0).then_inc(cst, 1)
            inv_root(ST_F1, 0)

        @block.tensor
        def _(pe):
            def mm3(dst, st, mv, start, stop):
                nc.tensor.matmul(dst, st[0], mv[0], start=start, stop=False)
                nc.tensor.matmul(dst, st[0], mv[1], start=False, stop=False)
                return nc.tensor.matmul(dst, st[1], mv[0], start=False, stop=stop)

            def weights(s, c0, c1):
                return w_hi[:, s, c0:c1], w_lo[:, s, c0:c1]

            def hidden(k, c0=0, c1=S):
                return h_hi[:, k, c0:c1], h_lo[:, k, c0:c1]

            def unit(pair, s):
                pe.wait_ge(w_lo_ok, 2 * pair + s + 1)

            def columns(n, squares):
                pe.wait_ge(ssum_ok, squares)
                for t in range(PT):
                    last = nc.tensor.matmul(ps[:, 6, t:t + 1], ssum[:, t * P:(t + 1) * P], ones[:, :],
                                            start=True, stop=True)
                last.then_inc(col_done, 1)

            def broadcast(n, which):
                pe.wait_ge(r_ok, n + 1)
                for t in range(PT):
                    last = nc.tensor.matmul(ps[:, 7, t * P:(t + 1) * P],
                                            rcol[:, which, t:t + 1].to_broadcast([P, P]), ident[:, :],
                                            start=True, stop=True)
                last.then_inc(bc_done, 1)

            pe.wait_ge(cst, 1)
            for s in range(2):
                unit(PAIR_KV, s)
                for t in range(PT):
                    for k4 in range(4):
                        k = 4 * s + k4
                        if t == 0:
                            pe.wait_ge(h_ready, k + 1)
                        last = mm3(ps[:, t, 0:256], hidden(k, t * P, (t + 1) * P),
                                   weights(s, k4 * 256, (k4 + 1) * 256), k == 0, k == KT - 1)
                last.then_inc(w_used, 1)
            columns(ST_A, SQ_BASE[NORM_A] + KT)
            for cb in range(2):
                for s in range(2):
                    unit(PAIR_Q + cb, s)
                    for t in range(PT):
                        if s == 0:
                            if cb == 0 and t == 2:
                                pe.wait_ge(var_ok, ST_A + 1)
                            if cb == 1:
                                pe.wait_ge(v_ok, t + 1)
                                pe.wait_ge(qn_ok, t + 1)
                        for k4 in range(4):
                            k = 4 * s + k4
                            last = mm3(ps[:, (0 if cb else 4) + t, :], hidden(k, t * P, (t + 1) * P),
                                       weights(s, k4 * S, (k4 + 1) * S), k == 0, k == KT - 1)
                    last.then_inc(w_used, 1)

            pe.wait_ge(c_in, 16 * 6)
            for g in range(10):
                if g < 4:
                    pe.wait_ge(qn_ok, 4 + g + 1)
                else:
                    pe.wait_ge(tp_ok, g - 3)
                pe.wait_ge(qrot_ok, 4 if g < 2 else (8 if g < 6 else 12))
                for t in range(PT):
                    src = kd[:, t, g, :, :].rearrange("p i d -> p (i d)") if g < 2 else \
                        qn[:, t, (g - 2) * P:(g - 1) * P]
                    last = nc.tensor.transpose(ps[:, 4 + g % 4, t * P:(t + 1) * P], src, ident[:, :])
                last.then_inc(tp_done, 1)

            def scores(g):
                c, n = GROUPS[g]
                if g < 2:
                    pe.wait_ge(qn_ok, 12)
                    pe.wait_ge(tp_ok, 10)
                    pe.wait_ge(cst, 8)
                else:
                    pe.wait_ge(e_ok, g - 1)
                nk = CHUNK if n == 0 else P
                keys = kTe if n % 2 == 0 else kTo
                for i in range(4):
                    par, j = i // 2, 4 * c + 2 * (i % 2)
                    last = nc.tensor.matmul(ps[:, g % 2, i * P:i * P + nk],
                                            qT[:, n, j:j + 2, :].rearrange("p j q -> p (j q)"),
                                            keys[:, par, c, n // 2, 0:nk], start=True, stop=True)
                last.then_inc(s_done, 1)

            def turn(g):
                pe.wait_ge(pn_ok, g + 1)
                if g >= 2:
                    pe.wait_ge(pt_ok, g - 1)
                for i in range(4):
                    last = nc.tensor.transpose(ps[:, 2 + g % 2, i * P:(i + 1) * P], pn[:, g % 2, i, :], ident[:, :])
                last.then_inc(pt_done, 1)

            def values(g):
                c, n = GROUPS[g]
                pe.wait_ge(pt_ok, g + 1)
                if g == 0:
                    pe.wait_ge(ve_ok, 2)
                else:
                    if g >= 2:
                        pe.wait_ge(alo_ok, g - 1)
                v = ve if n % 2 == 0 else va
                for par in range(2):
                    last = nc.tensor.matmul(ps[par * A_DH:(par + 1) * A_DH, 4 + g % 2, 0:4 * CHUNK],
                                            v[:, n // 2, c * A_DH:(c + 1) * A_DH],
                                            pT[:, g % 2, par * 256:(par + 1) * 256], start=True, stop=True)
                last.then_inc(pv_done, 1)

            NG = len(GROUPS)
            scores(0)
            for st in range(NG + 2):
                if st + 1 < NG:
                    scores(st + 1)
                if st < NG:
                    turn(st)
                if 1 <= st < NG + 1:
                    values(st - 1)

            for j in range(2):
                for s in range(2):
                    unit(PAIR_WO + j, s)
                    for e in range(2):
                        m = 4 * j + 2 * s + e
                        if m >= 4:
                            pe.wait_ge(xe_ok, XE_WO + m - 3)
                        for k in range(KT):
                            if m == 0 and k % 4 == 0:
                                pe.wait_ge(alo_ok, NCH * (k // 4 + 1))
                            last = mm3(ps[:, m % 4, :], weights(s, (e * KT + k) * P, (e * KT + k + 1) * P),
                                       (a_hi[:, k, :], a_lo[:, k, :]), k == 0, k == KT - 1)
                        last.then_inc(w_used if e else tile_done, 1)

            def mlp(layer):
                up, dn = PAIR_UP[layer], PAIR_DN[layer]
                norm = (NORM_F0, NORM_F1)[layer]

                def up_pair(j, s, first=False):
                    f = FT * layer + 2 * j + s
                    unit(up + j, s)
                    for ab in range(2):
                        if not first:
                            pe.wait_ge(u_ok, 2 * f - 3 + ab)
                        elif layer == 0:
                            pe.wait_ge(xe_ok, XE_WO + 5 + 2 * s + ab)
                        for k in range(KT):
                            if first and s == 0 and ab == 0:
                                pe.wait_ge(h_ready, KT * norm + k + 1)
                            c = (ab * KT + k) * P
                            last = mm3(ps[:, 2 * s + ab, :], weights(s, c, c + P), hidden(k), k == 0, k == KT - 1)
                        last.then_inc(w_used if ab else tile_done, 1)
                        if first and s == 0:
                            if ab == 0:
                                columns(ST_F1 if layer else ST_F0, SQ_BASE[norm] + KT)
                            else:
                                broadcast(ST_F1 if layer else ST_F0, 0)

                for s in range(2):
                    up_pair(0, s, first=True)
                with pe.Fori(1, FT // 2) as j:
                    for s in range(2):
                        up_pair(j, s)

                xe = (XE_DN0, XE_DN1)[layer]

                def down(m, e, wait_g=False):
                    if not (isinstance(m, int) and m < 2):
                        pe.wait_ge(xe_ok, xe + m - 1)
                    for s in range(2):
                        unit(dn + m, s)
                        for k11 in range(KH):
                            k = KH * s + k11
                            if wait_g and (k11 == 0 or k >= FT - 2):
                                pe.wait_ge(glo_ok, FT * layer + (KH if s == 0 else max(k + 1, FT - 2)))
                            last = mm3(ps[:, 4 + e, :], weights(s, k11 * P, (k11 + 1) * P),
                                       (g_hi[:, k, :], g_lo[:, k, :]), k == 0, k == FT - 1)
                        last.then_inc(w_used, 1)

                for e in range(2):
                    down(e, e, wait_g=(e == 0))
                with pe.Fori(1, KT // 2) as j:
                    for e in range(2):
                        down(2 * j + e, e)

            mlp(0)

            def qkvg(h, first):
                p0 = PAIR_RET if first else PAIR_RET + 4 * h - 1
                for s in range(2):
                    unit(p0, s)
                    for e in range(2):
                        if not first:
                            pe.wait_ge(ot_ok, 4 * (h - 1) + 2 * s + e + 1)
                        for k in range(KT):
                            if first and s == 0 and e == 0:
                                pe.wait_ge(h_ready, KT * NORM_R + k + 1)
                            last = mm3(ps[:, 2 * s + e, :], weights(s, (e * KT + k) * P, (e * KT + k + 1) * P),
                                       hidden(k), k == 0, k == KT - 1)
                        if e == 1:
                            last.then_inc(w_used, 1)
                        if s == 0 and e == 0:
                            if first:
                                columns(ST_R, SQ_BASE[NORM_R] + KT)
                            else:
                                pe.wait_ge(gx_ok, 4 * h)
                                columns(ST_HEAD + h - 1, SQ_HEAD + 4 * h)
                        if s == 0 and e == 1:
                            if first:
                                broadcast(ST_R, 0)
                            else:
                                broadcast(ST_HEAD + h - 1, 1)
                if not first:
                    project(h - 1, p0 + 1)
                pv = PAIR_RET + 1 if first else p0 + 2
                for s in range(2):
                    unit(pv, s)
                    for t in range(PT):
                        if s == 0:
                            if not first:
                                pe.wait_ge(xe_ok, XE_RO + KT * (h - 1) + 5 + t)
                            elif t == 0:
                                pe.wait_ge(bc_ok, BC_R + 1)
                        for k4 in range(4):
                            k = 4 * s + k4
                            last = mm3(ps[:, 4 + t, :], hidden(k, t * P, (t + 1) * P),
                                       weights(s, k4 * S, (k4 + 1) * S), k == 0, k == KT - 1)
                    last.then_inc(w_used, 1)
                pe.wait_ge(qk_ok, 4 * h + 4)
                for t in range(PT):
                    for d in range(2):
                        last = nc.tensor.matmul(ps[:, t, 0:S - t * P], qk[:, 2 + d, t * P:(t + 1) * P],
                                                qk[:, d, t * P:S], start=(d == 0), stop=(d == 1))
                    last.then_inc(rs_done, 1)
                for s in range(2):
                    unit(pv + 1, s)
                    for e in range(2):
                        m = 2 * s + e
                        pe.wait_ge(vr_ok, 4 * h + m + 1)
                        for k in range(KT):
                            last = mm3(ps[:, 4 + m, :], weights(s, (e * KT + k) * P, (e * KT + k + 1) * P),
                                       hidden(k), k == 0, k == KT - 1)
                    last.then_inc(w_used, 1)
                pe.wait_ge(pr_ok, 4 * h + 4)
                for m in range(RV_T):
                    for t in range(PT):
                        last = nc.tensor.matmul(ps[:, m, t * P:S], vr[:, t, m * P:(m + 1) * P], pr[:, t, 0:S - t * P],
                                                start=(t == 0), stop=(t == PT - 1))
                    last.then_inc(o_done, 1)

            def project(h, p):
                for s in range(2):
                    unit(p, s)
                    for e in range(4):
                        if s == 0 and e == 0:
                            pe.wait_ge(olo_ok, 4 * h + RV_T)
                        if s == 1:
                            pe.wait_ge(xe_ok, XE_RO + KT * h + e + 1)
                        for k in range(RV_T):
                            c = (e * RV_T + k) * P
                            last = mm3(ps[:, 4 + e, :], weights(s, c, c + P), (o_hi[:, k, :], o_lo[:, k, :]),
                                       k == 0, k == RV_T - 1)
                        last.then_inc(w_used if e == 3 else tile_done, 1)

            qkvg(0, True)
            with pe.Fori(1, R_HEADS) as h:
                qkvg(h, False)
            pe.wait_ge(gx_ok, 4 * R_HEADS)
            columns(ST_HEAD + R_HEADS - 1, SQ_HEAD + 4 * R_HEADS)
            broadcast(ST_HEAD + R_HEADS - 1, 1)
            project(R_HEADS - 1, PAIR_UP[1] - 1)

            mlp(1)


def _tables():
    def angles(base, rot, half):
        inv = (np.float64(np.float32(base)) ** (-np.arange(half) * 2.0 / rot)).astype(np.float32)
        return (np.arange(S, dtype=np.float32)[:, None] * inv[None, :]).astype(np.float64)

    half = A_ROT // 2
    a = angles(ROPE_THETA, A_ROT, half)
    cos, sin = np.cos(a), np.sin(a)
    rot_a = np.stack([np.concatenate([cos, cos], 1), np.concatenate([-sin, sin], 1)])
    rot_a = rot_a.reshape(2, PT, P, A_ROT).transpose(2, 0, 1, 3).astype(np.float32)
    b = angles(R_BASE, R_QK, R_QK // 2)
    rot_r = np.stack([np.cos(b).T, np.sin(b).T], 1).astype(np.float32)
    lg = np.log1p(-np.power(2.0, -5.0 - np.arange(R_HEADS)))
    key, query = np.arange(P)[:, None, None], np.arange(S)[None, None, :]
    decay = np.exp(lg[None, :, None] * np.abs(query - key)) * (query // CHUNK >= key // CHUNK) * R_QK ** -0.5
    return np.eye(P, dtype=np.float32), rot_a, rot_r, decay.astype(np.float32)


def kernel(x, norm1_g, norm2_g, attn_w_qkv, attn_w_o, attn_q_gain, attn_k_gain, attn_sinks,
           ret_w_in, ret_w_o, ffn_w_up, ffn_conv_w, ffn_conv_b, ffn_w_down):
    import concourse.bacc as bacc
    from concourse.bass_utils import run_bass_kernel_spmd

    A = np.asarray
    c = np.ascontiguousarray
    arrays = {}
    arrays["xT"] = c(A(x)[0].T.reshape(KT, P, S))

    def moving(w, cols):
        return w.reshape(2, 4, P, cols).transpose(0, 2, 1, 3).reshape(2, P, 4 * cols)

    def stationary(w, kt, per):
        n = w.shape[1] // P
        return w.reshape(kt, P, n // per, per, P).transpose(2, 1, 3, 0, 4).reshape(n // per, P, per * kt * P)

    wqkv = A(attn_w_qkv)[0]
    arrays["w_kv"] = c(moving(wqkv[:, D:], 256))
    arrays["w_q"] = c(np.concatenate([moving(wqkv[:, 0:S], S), moving(wqkv[:, S:D], S)]))
    arrays["w_ao"] = c(stationary(A(attn_w_o)[0], KT, 2))
    for layer in range(2):
        wu = A(ffn_w_up)[layer].reshape(KT, P, 2, FT, P)
        wu_arr = c(wu.transpose(3, 1, 2, 0, 4).reshape(FT, P, UW))
        wd = A(ffn_w_down)[layer].reshape(2, KH, P, KT, P)
        wd_arr = c(wd.transpose(3, 0, 2, 1, 4).reshape(2 * KT, P, DW))
        arrays[f"w_up{layer}"], arrays[f"w_dn{layer}"] = wu_arr, wd_arr
    wr, wo = A(ret_w_in)[0], A(ret_w_o)[0]
    units = []
    for h in range(R_HEADS + 1):
        if h < R_HEADS:
            units += [stationary(wr[:, i * D + h * R_QK:i * D + (h + 1) * R_QK], KT, 2) for i in range(2)]
        if h > 0:
            units.append(stationary(wo[(h - 1) * R_V:h * R_V], RV_T, 4))
        if h < R_HEADS:
            units.append(moving(wr[:, 2 * D + h * R_V:2 * D + (h + 1) * R_V], R_V))
            units.append(stationary(wr[:, 4 * D + h * R_V:4 * D + (h + 1) * R_V], KT, 2))
    arrays["w_ret"] = c(np.concatenate(units))
    arrays["gains"] = c(np.stack([A(norm1_g)[0], A(norm2_g)[0], A(norm1_g)[1], A(norm2_g)[1]])
                        .reshape(4, KT, P).transpose(2, 0, 1))
    cw = np.concatenate([A(ffn_conv_w)[:, :, 0, :], A(ffn_conv_b)[:, None, :]], 1)
    arrays["conv"] = c(cw.reshape(2, 4, 2, FT, P).transpose(4, 0, 3, 2, 1).reshape(P, 2, FT, 8))
    arrays["gain_qk"] = c(np.broadcast_to(np.stack([A(attn_q_gain)[0], A(attn_k_gain)[0]])[None], (P, 2, A_DH)))
    sk = A(attn_sinks)[0].reshape(A_KVH, 2, 2, 2)
    sk = sk.transpose(2, 0, 3, 1).reshape(2, 1, A_KVH, 4)
    arrays["sinks"] = c(np.broadcast_to(sk, (2, CHUNK, A_KVH, 4)).reshape(P, A_KVH, 4))
    arrays["ident"], arrays["rot_a"], arrays["rot_r"], arrays["decay"] = (c(t) for t in _tables())

    nc = bacc.Bacc("TRN2", target_bir_lowering=False, num_devices=1)
    args = [nc.dram_tensor(f"in_{n}", a.shape, F32, kind="ExternalInput").ap() for n, a in arrays.items()]
    out = nc.dram_tensor("out", (KT, P, S), F32, kind="ExternalOutput").ap()
    names = list(arrays)
    by = dict(zip(names, args))
    trunk(nc, by["xT"], by["w_kv"], by["w_q"], by["w_ao"], by["w_up0"], by["w_dn0"], by["w_ret"], by["w_up1"],
          by["w_dn1"], by["gains"], by["conv"], by["gain_qk"], by["sinks"], by["ident"], by["rot_a"],
          by["rot_r"], by["decay"], out)
    r = run_bass_kernel_spmd(nc, [{f"in_{n}": a for n, a in arrays.items()}], core_ids=[0])
    got = r.results[0]["out"]
    return np.ascontiguousarray(got.reshape(D, S).T).reshape(1, S, D)
```

```python
from contextlib import ExitStack

import numpy as np

import concourse.bass as bass
from concourse import mybir

F32 = mybir.dt.float32
F32R = mybir.dt.float32r
ALU = mybir.AluOpType
ACT = mybir.ActivationFunctionType
AX = mybir.AxisListType

P = 128
D = 1024
S = 512
KT = D // P
PT = S // P
EPS = 1e-6
CHUNK = 64
NCH = S // CHUNK
A_HEADS, A_DH, A_KVH = 16, 64, 2
A_ROT = A_DH // 4
A_SCALE = A_DH ** -0.5
ROPE_THETA = 500000.0
R_HEADS = 4
R_QK = D // R_HEADS
R_V = 2 * D // R_HEADS
R_BASE = 10000.0
RV_T = R_V // P
D_FF = 2816
FT = D_FF // P
KH = FT // 2
UW = 2048
DW = KH * P
KVW = 4 * 256

PAIR_KV = 0
PAIR_Q = 1
PAIR_WO = 3
PAIR_UP = (5, 40)
PAIR_DN = (5 + FT // 2, 40 + FT // 2)
PAIR_RET = PAIR_DN[0] + KT
N_PAIRS = PAIR_DN[1] + KT
assert PAIR_RET == 24 and PAIR_RET + 4 * R_HEADS == PAIR_UP[1]

NORM_A, NORM_F0, NORM_R, NORM_F1 = range(4)
SQ_BASE = (0, KT, 2 * KT, 3 * KT + R_HEADS * RV_T)
SQ_HEAD = 3 * KT
XE_WO, XE_DN0 = 0, KT
XE_RO = 2 * KT
XE_DN1 = 2 * KT + R_HEADS * KT
TD_QKV = 0
TD_WO = 9
TD_UP0 = TD_WO + 4
TD_RO = TD_UP0 + FT
TD_UP1 = TD_RO + 6 * R_HEADS
ST_A, ST_F0, ST_R, ST_HEAD, ST_F1 = 0, 1, 2, 3, 3 + R_HEADS
BC_F0, BC_R, BC_HEAD, BC_F1 = 0, 1, 2, 2 + R_HEADS


def trunk(nc, xT, w_kv, w_q, w_ao, w_up0, w_dn0, w_ret, w_up1, w_dn1, gains, conv, gain_qk, sinks,
          ident_d, rot_a, rot_r, decay, out):
    ctx = ExitStack()
    with ctx:
        def sb(name, shape, dt=F32, scope=ctx):
            return scope.enter_context(nc.sbuf_tensor(name, shape, dt))

        def sem(name):
            return ctx.enter_context(nc.semaphore(name))

        x = sb("x", [P, KT, S])
        h_hi = sb("h_hi", [P, KT, S], F32R)
        h_lo = sb("h_lo", [P, KT, S], F32R)
        raw = sb("raw", [P, 2, UW])
        w_hi = sb("w_hi", [P, 2, UW], F32R)
        w_lo = sb("w_lo", [P, 2, UW], F32R)
        gain = sb("gain", [P, 4, KT])
        cvec = sb("cvec", [P, 2, FT, 8])
        ident = sb("ident", [P, P])
        ones = sb("ones", [P, 1])
        mhalf = sb("mhalf", [P, 8])
        sq = sb("sq", [P, 2, S])
        ssum = sb("ssum", [P, S])
        var = sb("var", [P, 2, PT])
        rcol = sb("rcol", [P, 2, PT])
        rbc = sb("rbc", [P, 2, S])
        ps = ctx.enter_context(nc.psum_tensor("ps", [P, 8, S], F32))

        att = ExitStack()
        qn = sb("qn", [P, PT, D], scope=att)
        kd = sb("kd", [P, PT, A_KVH, 2, A_DH], scope=att)
        va = sb("va", [P, PT, A_KVH * A_DH], scope=att)
        ve = sb("ve", [P, PT, A_KVH * A_DH], scope=att)
        qT = sb("qT", [P, NCH, KT, CHUNK], scope=att)
        kTo = sb("kTo", [P, 2, A_KVH, PT, P], scope=att)
        kTe = sb("kTe", [P, 2, A_KVH, PT, P], scope=att)
        a_hi = sb("a_hi", [P, KT, S], F32R, scope=att)
        a_lo = sb("a_lo", [P, KT, S], F32R, scope=att)
        sqq = sb("sqq", [P, 2, S], scope=att)
        qvar = sb("qvar", [P, 2, 8], scope=att)
        qss = sb("qss", [P, 2, 8], scope=att)
        qs = sb("qs", [P, 2, 8], scope=att)
        gqk = sb("gqk", [P, 2, A_DH], scope=att)
        rota = sb("rota", [P, 2, PT, A_ROT], scope=att)
        ra = sb("ra", [P, 8, A_ROT], scope=att)
        rb = sb("rb", [P, 8, A_ROT], scope=att)
        sink = sb("sink", [P, A_KVH, 4], scope=att)
        nsink = sb("nsink", [P, A_KVH, 4], scope=att)
        mx = sb("mx", [P, 2, 4], scope=att)
        nm = sb("nm", [P, 2, 4], scope=att)
        dm = sb("dm", [P, 2, 4], scope=att)
        es = sb("es", [P, 2, 4], scope=att)
        sm = sb("sm", [P, 2, 4], scope=att)
        den = sb("den", [P, 2, 4], scope=att)
        rd = sb("rd", [P, 2, 4], scope=att)
        ex = sb("ex", [P, 2, 4, P], scope=att)
        pn = qn[:, 0:2, 0:S].rearrange("p r (i k) -> p r i k", i=4)
        pT = qn[:, 2:4, 0:S]
        att.close()

        ffn = ExitStack()
        g_hi = sb("g_hi", [P, FT, S], F32R, scope=ffn)
        g_lo = sb("g_lo", [P, FT, S], F32R, scope=ffn)
        u = sb("u", [P, 2, S + 2], scope=ffn)
        y = sb("y", [P, 2, S], scope=ffn)
        gp = sb("gp", [P, S], scope=ffn)
        ffn.close()

        ret = ExitStack()
        rt = sb("rt", [P, 4, S], scope=ret)
        qk_hi = sb("qk_hi", [P, 4, S], F32R, scope=ret)
        qk_lo = sb("qk_lo", [P, 4, S], F32R, scope=ret)
        v_hi = sb("v_hi", [P, PT, R_V], F32R, scope=ret)
        v_lo = sb("v_lo", [P, PT, R_V], F32R, scope=ret)
        pf = sb("pf", [P, 2, S], scope=ret)
        p_hi = sb("p_hi", [P, PT, S], F32R, scope=ret)
        p_lo = sb("p_lo", [P, PT, S], F32R, scope=ret)
        sg = sb("sg", [P, RV_T, S], scope=ret)
        o_hi = sb("o_hi", [P, RV_T, S], F32R, scope=ret)
        o_lo = sb("o_lo", [P, RV_T, S], F32R, scope=ret)
        csr = sb("csr", [P, 2, S], scope=ret)
        dec = sb("dec", [P, R_HEADS, S], scope=ret)
        tab = rt[:, 0:2, :]
        ret.close()

        x_in = [sem(f"x_in{k}") for k in range(KT)]
        g_in = sem("g_in")
        c_in = sem("c_in")
        r_in = sem("r_in")
        o_out = sem("o_out")
        cst = sem("cst")
        w_loaded = [sem("w_loaded0"), sem("w_loaded1")]
        w_hi_ok, w_lo_ok, w_used = sem("w_hi_ok"), sem("w_lo_ok"), sem("w_used")
        tile_done = sem("tile_done")
        h_hi_ok, h_ready = sem("h_hi_ok"), sem("h_ready")
        sq_ok, ssum_ok = sem("sq_ok"), sem("ssum_ok")
        col_done, var_ok, r_ok, bc_done, bc_ok = (sem(n) for n in ("col_done", "var_ok", "r_ok", "bc_done", "bc_ok"))
        xe_ok = sem("xe_ok")
        v_ok, ve_ok = sem("v_ok"), sem("ve_ok")
        qsq_ok, qss_ok, qvar_ok, qs_ok, qn_ok, qrot_ok = (sem(n) for n in (
            "qsq_ok", "qss_ok", "qvar_ok", "qs_ok", "qn_ok", "qrot_ok"))
        pool_step = sem("pool_step")
        tp_done, tp_ok = sem("tp_done"), sem("tp_ok")
        s_done, mx_ok, nm_ok, dm_ok, ex_ok, den_ok, rd_ok, pn_ok = (sem(n) for n in (
            "s_done", "mx_ok", "nm_ok", "dm_ok", "ex_ok", "den_ok", "rd_ok", "pn_ok"))
        nsink_ok = sem("nsink_ok")
        pz_ok = sem("pz_ok")
        pt_done, pt_ok, pv_done, ahi_ok, alo_ok = (sem(n) for n in (
            "pt_done", "pt_ok", "pv_done", "ahi_ok", "alo_ok"))
        u_ok, yb_ok, y1_ok, y_ok, ge_ok, gp_ok, ghi_ok, glo_ok = (sem(n) for n in (
            "u_ok", "yb_ok", "y1_ok", "y_ok", "ge_ok", "gp_ok", "ghi_ok", "glo_ok"))
        csr_ok, rt_ok, rot_ok, qhi_ok, qlo_ok, vhi_ok, vlo_ok = (sem(n) for n in (
            "csr_ok", "rt_ok", "rot_ok", "qhi_ok", "qlo_ok", "vhi_ok", "vlo_ok"))
        rs_done, pf_ok, phi_ok, plo_ok, gx_ok, sg_ok = (sem(n) for n in (
            "rs_done", "pf_ok", "phi_ok", "plo_ok", "gx_ok", "sg_ok"))
        o_done, ot_ok, ohi_ok, olo_ok, pj_ok = (sem(n) for n in ("o_done", "ot_ok", "ohi_ok", "olo_ok", "pj_ok"))

        block = ctx.enter_context(nc.Block())

        def bank_of(n):
            return (n % PT) + (4 if 4 <= n < 8 else 0)

        def item_sums(eng, n):
            if n % PT < PT - 1:
                eng.wait_ge(tile_done, TD_QKV + 3 * (n // PT) + n % PT + 1)
            else:
                eng.wait_ge(w_used, 2 * (n // PT + 1))

        def score_bank(g):
            return (6, 7, 0)[g % 3]

        def turn_bank(g):
            return 4 + g % 4 if g < 6 else 1

        GROUPS = [(g // NCH, g % NCH) for g in range(A_KVH * NCH)]

        @block.sync
        def _(sp):
            def load(src, pair, s, cols, first=False):
                if not first:
                    sp.wait_ge(w_lo_ok, 2 * pair + s - 1)
                sp.dma_start(raw[:, s, 0:cols], src).then_inc(w_loaded[s], 16)

            for k in range(KT):
                sp.dma_start(x[:, k, :], xT[k]).then_inc(x_in[k], 16)
                if k == 1:
                    load(w_kv[0], PAIR_KV, 0, KVW, first=True)
                if k == 5:
                    load(w_kv[1], PAIR_KV, 1, KVW, first=True)
            for cb in range(2):
                for s in range(2):
                    load(w_q[2 * cb + s], PAIR_Q + cb, s, UW)
            for j in range(2):
                for s in range(2):
                    load(w_ao[2 * j + s], PAIR_WO + j, s, UW)

            def rows(src, i):
                return src[bass.ds(i, 1), :, :].rearrange("o p f -> (o p) f")

            def mlp(layer, w_up, w_dn):
                with sp.Fori(0, FT // 2) as j:
                    for s in range(2):
                        load(rows(w_up, 2 * j + s), PAIR_UP[layer] + j, s, UW)
                with sp.Fori(0, KT) as j:
                    for s in range(2):
                        load(rows(w_dn, 2 * j + s), PAIR_DN[layer] + j, s, DW)

            mlp(0, w_up0, w_dn0)
            with sp.Fori(0, 4 * R_HEADS) as j:
                for s in range(2):
                    load(rows(w_ret, 2 * j + s), PAIR_RET + j, s, UW)
            mlp(1, w_up1, w_dn1)
            for m in range(KT):
                sp.wait_ge(xe_ok, XE_DN1 + m + 1)
                sp.dma_start(out[m], x[:, m, :]).then_inc(o_out, 16)
            sp.wait_ge(o_out, 16 * KT)

        @block.scalar
        def _(act):
            act.dma_start(gain[:, :, :], gains).then_inc(g_in, 16)

            def split(pair, s, cols, first=False):
                act.wait_ge(w_loaded[s], 16 * (pair + 1))
                if not first:
                    act.wait_ge(w_used, 2 * pair + s - 1)
                nc.scalar.activation(w_hi[:, s, 0:cols], raw[:, s, 0:cols], ACT.Copy).then_inc(w_hi_ok, 1)

            def hi_part(norm, m):
                nc.scalar.activation(h_hi[:, m, :], x[:, m, :], ACT.Copy,
                                     scale=gain[:, norm, m:m + 1]).then_inc(h_hi_ok, 1)

            def hi_tile(norm, m):
                hi_part(norm, m)
                square(SQ_BASE[norm], m, x[:, m, :])

            def square(base, m, src):
                n = base + m
                if not (isinstance(n, int) and n < 2):
                    act.wait_ge(ssum_ok, n - 1)
                nc.scalar.activation(sq[:, m % 2, :], src, ACT.Square).then_inc(sq_ok, 1)

            def broadcast_out(n, which):
                act.wait_ge(bc_done, n + 1)
                nc.scalar.activation(rbc[:, which, :], ps[:, 7, :], ACT.Copy).then_inc(bc_ok, 1)

            act.wait_ge(g_in, 16)
            for k in range(KT):
                act.wait_ge(x_in[k], 16)
                hi_part(NORM_A, k)
                if k == 1:
                    split(PAIR_KV, 0, KVW, first=True)
                if k == 5:
                    split(PAIR_KV, 1, KVW, first=True)
            for k in range(KT):
                square(SQ_BASE[NORM_A], k, x[:, k, :])
                if k == 3:
                    split(PAIR_Q, 0, UW)
            split(PAIR_Q, 1, UW)

            def q_square(n, width):
                t = n % PT
                item_sums(act, n)
                if n >= 2:
                    act.wait_ge(qss_ok, n - 1)
                nc.scalar.activation(sqq[:, n % 2, 0:width], ps[:, bank_of(n), 0:width], ACT.Square,
                                     scale=rcol[:, 0, t:t + 1]).then_inc(qsq_ok, 1)

            def turned_out(g):
                act.wait_ge(tp_done, g + 1)
                b = ps[:, turn_bank(g), :]
                if g < 2:
                    own = b.rearrange("p (t c) -> p t c", c=P)
                    for par in range(2):
                        rows = slice(par * A_DH, (par + 1) * A_DH)
                        nc.scalar.activation(kTo[rows, par, g, :, :], own[rows], ACT.Copy)
                        nc.scalar.activation(kTe[rows, par, g, :, 0:CHUNK], own[rows, :, 0:CHUNK], ACT.Copy)
                        last = nc.scalar.activation(kTe[rows, par, g, 1:PT, CHUNK:P], own[rows, 0:PT - 1, CHUNK:P],
                                                    ACT.Copy)
                    last.then_inc(tp_ok, 1)
                else:
                    nc.scalar.activation(qT[:, :, g - 2, :], b.rearrange("p (n c) -> p n c", c=CHUNK),
                                         ACT.Copy).then_inc(tp_ok, 1)

            act.wait_ge(r_ok, ST_A + 1)
            for t in range(PT):
                item_sums(act, t)
                nc.scalar.activation(va[:, t, :], ps[:, t, P:2 * P], ACT.Copy,
                                     scale=rcol[:, 0, t:t + 1]).then_inc(v_ok, 1)
                q_square(t, P)
            split(PAIR_Q + 1, 0, UW)
            for n in range(4, 8):
                q_square(n, S)
            split(PAIR_Q + 1, 1, UW)
            split(PAIR_WO, 0, UW)
            turned_out(0)
            turned_out(1)
            for n in range(8, 12):
                q_square(n, S)
                turned_out(n - 6)
            split(PAIR_WO, 1, UW)

            def exps(g):
                _, n = GROUPS[g]
                nk = CHUNK if n == 0 else P
                r = g % 2
                act.wait_ge(dm_ok, g + 1)
                if g >= 2:
                    act.wait_ge(pn_ok, g - 1)
                for i in range(4):
                    nc.scalar.activation(ex[:, r, i, 0:nk], ps[:, score_bank(g), i * P:i * P + nk], ACT.Exp,
                                         scale=A_SCALE, bias=nm[:, r, i:i + 1], accum_out=sm[:, r, i:i + 1])
                nc.scalar.activation(es[:, r, :], dm[:, r, :], ACT.Exp).then_inc(ex_ok, 1)

            def heads_out(g):
                c, n = GROUPS[g]
                act.wait_ge(pv_done, g + 1)
                nc.scalar.activation(a_hi[:, 4 * c:4 * c + 4, n * CHUNK:(n + 1) * CHUNK],
                                     ps[:, 4 + g % 2, 0:4 * CHUNK].rearrange("p (j q) -> p j q", q=CHUNK),
                                     ACT.Copy).then_inc(ahi_ok, 1)

            NG = len(GROUPS)
            for st in range(NG + 2):
                if st < NG:
                    exps(st)
                if 1 <= st <= 4:
                    turned_out(5 + st)
                if st >= 2:
                    heads_out(st - 2)

            for j in range(2):
                for s in range(2):
                    for e in range(2):
                        m = 4 * j + 2 * s + e
                        act.wait_ge(xe_ok, XE_WO + m + 1)
                        hi_tile(NORM_F0, m)
                        if e == 0:
                            split(PAIR_WO + j + 1, s, UW)

            def mlp(layer, last_layer):
                up, dn = PAIR_UP[layer], PAIR_DN[layer]

                def up_pair(j, s, cols, first=False):
                    i = 2 * j + s
                    f = FT * layer + i
                    if first and s == 0:
                        broadcast_out(BC_F1 if layer else BC_F0, 0)
                    for ab in range(2):
                        act.wait_ge(u_ok, 2 * f + ab + 1)
                        c = cvec[:, layer, bass.ds(i, 1), 4 * ab + 2:4 * ab + 4].rearrange("p o f -> p (o f)")
                        nc.scalar.activation(y[:, ab, :], u[:, ab, 2:S + 2], ACT.Identity,
                                             scale=c[:, 0:1], bias=c[:, 1:2]).then_inc(yb_ok, 1)
                    split(up + j + 1, s, cols)
                    act.wait_ge(y_ok, 2 * f + 1)
                    nc.scalar.activation(y[:, 0, :], y[:, 0, :], ACT.Gelu).then_inc(ge_ok, 1)
                    act.wait_ge(gp_ok, f + 1)
                    nc.scalar.activation(g_hi[:, bass.ds(i, 1), :].rearrange("p o f -> p (o f)"), gp[:, :],
                                         ACT.Copy).then_inc(ghi_ok, 1)

                for s in range(2):
                    up_pair(0, s, UW, first=True)
                with act.Fori(1, FT // 2 - 1) as j:
                    for s in range(2):
                        up_pair(j, s, UW)
                for s in range(2):
                    up_pair(FT // 2 - 1, s, DW)

                def down(m, e, cols):
                    for s in range(2):
                        if cols:
                            split(dn + m + 1, s, cols)
                    if not last_layer:
                        act.wait_ge(ssum_ok, SQ_BASE[NORM_R] + m - 1)
                        act.wait_ge(xe_ok, XE_DN0 + m + 1)
                        gv = gain[:, NORM_R, bass.ds(m, 1)]
                        nc.scalar.activation(h_hi[:, bass.ds(m, 1), :].rearrange("p o f -> p (o f)"),
                                             x[:, bass.ds(m, 1), :].rearrange("p o f -> p (o f)"), ACT.Copy,
                                             scale=gv).then_inc(h_hi_ok, 1)
                        nc.scalar.activation(sq[:, e, :], x[:, bass.ds(m, 1), :].rearrange("p o f -> p (o f)"),
                                             ACT.Square).then_inc(sq_ok, 1)

                with act.Fori(0, KT // 2 - 1) as j:
                    for e in range(2):
                        down(2 * j + e, e, DW)
                down(KT - 2, 0, DW)
                down(KT - 1, 1, 0 if last_layer else UW)

            mlp(0, False)

            def qkvg(h, first):
                p0 = PAIR_RET if first else PAIR_RET + 4 * h - 1
                pv = PAIR_RET + 1 if first else p0 + 2
                split(p0 + 1, 0, UW)
                if not first:
                    broadcast_out(BC_HEAD + h - 1, 1)
                rotated(h, 0)
                split(p0 + 1, 1, UW)
                rotated(h, 1)
                if not first:
                    for s in range(2):
                        split(p0 + 2, s, UW)
                split(pv + 1, 0, UW)
                act.wait_ge(w_used, 2 * pv + 2)
                for t in range(PT):
                    nc.scalar.activation(v_hi[:, t, :], ps[:, 4 + t, :], ACT.Copy,
                                         scale=rcol[:, 0, t:t + 1]).then_inc(vhi_ok, 1)
                split(pv + 1, 1, UW)
                for t in range(PT):
                    w = S - t * P
                    act.wait_ge(pf_ok, 4 * h + t + 1)
                    nc.scalar.activation(p_hi[:, t, 0:w], pf[:, t % 2, 0:w], ACT.Copy).then_inc(phi_ok, 1)
                for s in range(2):
                    for e in range(2):
                        m = 2 * s + e
                        act.wait_ge(gx_ok, 4 * h + m + 1)
                        nc.scalar.activation(sg[:, m, :], sg[:, m, :], ACT.Silu).then_inc(sg_ok, 1)
                    split(pv + 2, s, UW)
                for m in range(RV_T):
                    act.wait_ge(ot_ok, 4 * h + m + 1)
                    nc.scalar.activation(o_hi[:, m, :], sg[:, m, :], ACT.Copy).then_inc(ohi_ok, 1)
                    square(SQ_HEAD + 4 * h, m, ps[:, m, :])

            def rotated(h, s):
                for i in range(2):
                    act.wait_ge(rot_ok, 4 * h + 2 * s + i + 1)
                    nc.scalar.activation(qk_hi[:, 2 * s + i, :], rt[:, 2 * i, :], ACT.Copy).then_inc(qhi_ok, 1)

            act.wait_ge(w_used, 2 * PAIR_RET)
            act.dma_start(tab, rot_r).then_inc(r_in, 16)
            act.dma_start(dec[:, :, :], decay).then_inc(r_in, 16)
            broadcast_out(BC_R, 0)
            qkvg(0, True)
            with act.Fori(1, R_HEADS) as h:
                qkvg(h, False)
            broadcast_out(BC_HEAD + R_HEADS - 1, 1)
            for s in range(2):
                split(PAIR_UP[1], s, UW)
                for e in range(4):
                    m = 4 * s + e
                    act.wait_ge(xe_ok, XE_RO + KT * (R_HEADS - 1) + m + 1)
                    hi_tile(NORM_F1, m)

            mlp(1, True)

        @block.vector
        def _(dve):
            def split(pair, s, cols):
                dve.wait_ge(w_hi_ok, 2 * pair + s + 1)
                nc.vector.tensor_tensor(w_lo[:, s, 0:cols], raw[:, s, 0:cols], w_hi[:, s, 0:cols].bitcast(F32),
                                        ALU.subtract).then_inc(w_lo_ok, 1)

            def lo_tile(norm, m, xm, hm, lm, g):
                dve.wait_ge(h_hi_ok, KT * norm + m + 1)
                nc.vector.scalar_tensor_tensor(lm, xm, g, hm.bitcast(F32), ALU.mult,
                                               ALU.subtract).then_inc(h_ready, 1)

            def lo_static(norm, m):
                lo_tile(norm, m, x[:, m, :], h_hi[:, m, :], h_lo[:, m, :], gain[:, norm, m:m + 1])

            def variance(n, which, width):
                dve.wait_ge(col_done, n + 1)
                nc.vector.tensor_scalar(var[:, which, :], ps[:, 6, 0:PT], 1.0 / width, EPS, ALU.mult,
                                        ALU.add).then_inc(var_ok, 1)

            def add_tile(m, bank):
                nc.vector.tensor_tensor(x[:, m, :], ps[:, bank, :], x[:, m, :], ALU.add).then_inc(xe_ok, 1)

            for k in range(KT):
                lo_static(NORM_A, k)
                if k == 1:
                    split(PAIR_KV, 0, KVW)
                if k == 5:
                    split(PAIR_KV, 1, KVW)
            split(PAIR_Q, 0, UW)
            variance(ST_A, 0, D)
            split(PAIR_Q, 1, UW)

            def q_var(n, heads):
                dve.wait_ge(qsq_ok, n + 1)
                nc.vector.tensor_reduce(qss[:, n % 2, 0:heads],
                                        sqq[:, n % 2, 0:heads * A_DH].rearrange("p (h d) -> p h d", d=A_DH),
                                        AX.X, ALU.add).then_inc(qss_ok, 1)
                dve.wait_ge(qss_ok, n + 1)
                nc.vector.tensor_scalar(qvar[:, n % 2, 0:heads], qss[:, n % 2, 0:heads], 1.0 / A_DH, EPS,
                                        ALU.mult, ALU.add).then_inc(qvar_ok, 1)

            def q_norm(n, heads):
                t = n % PT
                src = ps[:, bank_of(n), 0:heads * A_DH].rearrange("p (h d) -> p h d", d=A_DH)
                if n < 4:
                    dst = kd[:, t, :, 0, :]
                else:
                    cb = (n - 4) // 4
                    dst = qn[:, t, cb * S:(cb + 1) * S].rearrange("p (h d) -> p h d", d=A_DH)
                dve.wait_ge(qs_ok, n + 1)
                nc.vector.scalar_tensor_tensor(dst, src, rcol[:, 0, t:t + 1],
                                               qs[:, n % 2, 0:heads].unsqueeze(2).to_broadcast([P, heads, A_DH]),
                                               ALU.mult, ALU.mult).then_inc(qn_ok, 1)

            def q_items(items, heads):
                for n in items:
                    q_var(n, heads)
                    q_norm(n, heads)

            q_items(range(0, 4), 2)
            split(PAIR_Q + 1, 0, UW)
            q_items(range(4, 8), 8)
            split(PAIR_Q + 1, 1, UW)
            dve.wait_ge(c_in, 16 * 5)
            nc.vector.tensor_scalar(nsink[:, :, :], sink[:, :, :], -1.0, None, ALU.mult).then_inc(nsink_ok, 1)
            split(PAIR_WO, 0, UW)
            q_items(range(8, 12), 8)
            dve.wait_ge(nsink_ok, 1)

            def softmax_top(g):
                c, n = GROUPS[g]
                nk = CHUNK if n == 0 else P
                r = g % 2
                dve.wait_ge(s_done, g + 1)
                nc.vector.tensor_reduce(mx[:, r, :],
                                        ps[:, score_bank(g), :].rearrange("p (i k) -> p i k", k=P)[:, :, 0:nk],
                                        AX.X, ALU.max).then_inc(mx_ok, 1)
                dve.wait_ge(mx_ok, g + 1)
                nc.vector.scalar_tensor_tensor(nm[:, r, :], mx[:, r, :], -A_SCALE, nsink[:, c, :], ALU.mult,
                                               ALU.min).then_inc(nm_ok, 1)
                dve.wait_ge(nm_ok, g + 1)
                nc.vector.tensor_tensor(dm[:, r, :], sink[:, c, :], nm[:, r, :], ALU.add).then_inc(dm_ok, 1)

            def softmax_bottom(g):
                r = g % 2
                dve.wait_ge(ex_ok, g + 1)
                nc.vector.tensor_tensor(den[:, r, :], sm[:, r, :], es[:, r, :], ALU.add).then_inc(den_ok, 1)
                dve.wait_ge(den_ok, g + 1)
                nc.vector.reciprocal(rd[:, r, :], den[:, r, :]).then_inc(rd_ok, 1)

            def probs_out(g):
                dve.wait_ge(pt_done, g + 1)
                nc.vector.tensor_copy(pT[:, g % 2, :], ps[:, 2 + g % 2, :]).then_inc(pt_ok, 1)

            def heads_lo(g):
                c, n = GROUPS[g]
                dst = (slice(None), slice(4 * c, 4 * c + 4), slice(n * CHUNK, (n + 1) * CHUNK))
                dve.wait_ge(ahi_ok, g + 1)
                nc.vector.tensor_tensor(a_lo[dst], ps[:, 4 + g % 2, 0:4 * CHUNK].rearrange("p (j q) -> p j q", q=CHUNK),
                                        a_hi[dst].bitcast(F32), ALU.subtract).then_inc(alo_ok, 1)

            NG = len(GROUPS)
            softmax_top(0)
            for st in range(NG + 2):
                if st + 1 < NG:
                    softmax_top(st + 1)
                if st < NG:
                    softmax_bottom(st)
                if 1 <= st < NG + 1:
                    probs_out(st - 1)
                if st == 0:
                    split(PAIR_WO, 1, UW)
                if st >= 2:
                    heads_lo(st - 2)

            for j in range(2):
                for s in range(2):
                    for e in range(2):
                        m = 4 * j + 2 * s + e
                        if e == 0:
                            dve.wait_ge(tile_done, TD_WO + 2 * j + s + 1)
                        else:
                            dve.wait_ge(w_used, 2 * (PAIR_WO + j) + s + 1)
                        add_tile(m, m % 4)
                        if m > 0:
                            lo_static(NORM_F0, m - 1)
                        if e == 1:
                            split(PAIR_WO + j + 1, s, UW)
            lo_static(NORM_F0, KT - 1)

            def mlp(layer, last_layer):
                up, dn = PAIR_UP[layer], PAIR_DN[layer]
                td = (TD_UP0, TD_UP1)[layer]

                def up_pair(j, s, cols, first=False):
                    i = 2 * j + s
                    f = FT * layer + i
                    c = cvec[:, layer, bass.ds(i, 1), :].rearrange("p o f -> p (o f)")
                    if first and s == 0:
                        variance(ST_F1 if layer else ST_F0, 0, D)
                        dve.wait_ge(cst, 9 + layer)
                        dve.wait_ge(bc_ok, (BC_F1 if layer else BC_F0) + 1)
                    dve.wait_ge(tile_done, td + i + 1)
                    nc.vector.tensor_tensor(u[:, 0, 2:S + 2], ps[:, 2 * s, :], rbc[:, 0, :], ALU.mult).then_inc(u_ok, 1)
                    dve.wait_ge(w_used, 2 * (up + j) + s + 1)
                    nc.vector.tensor_tensor(u[:, 1, 2:S + 2], ps[:, 2 * s + 1, :], rbc[:, 0, :],
                                            ALU.mult).then_inc(u_ok, 1)
                    for ab in range(2):
                        dve.wait_ge(yb_ok, 2 * f + ab + 1)
                        nc.vector.scalar_tensor_tensor(y[:, ab, :], u[:, ab, 1:S + 1], c[:, 4 * ab + 1:4 * ab + 2],
                                                       y[:, ab, :], ALU.mult, ALU.add).then_inc(y1_ok, 1)
                    for ab in range(2):
                        dve.wait_ge(y1_ok, 2 * f + ab + 1)
                        nc.vector.scalar_tensor_tensor(y[:, ab, :], u[:, ab, 0:S], c[:, 4 * ab:4 * ab + 1],
                                                       y[:, ab, :], ALU.mult, ALU.add).then_inc(y_ok, 1)
                    split(up + j + 1, s, cols)
                    dve.wait_ge(ge_ok, f + 1)
                    dve.wait_ge(y_ok, 2 * f + 2)
                    nc.vector.tensor_tensor(gp[:, :], y[:, 0, :], y[:, 1, :], ALU.mult).then_inc(gp_ok, 1)
                    dve.wait_ge(ghi_ok, f + 1)
                    gi = (slice(None), bass.ds(i, 1), slice(None))
                    nc.vector.tensor_tensor(g_lo[gi].rearrange("p o f -> p (o f)"), gp[:, :],
                                            g_hi[gi].rearrange("p o f -> p (o f)").bitcast(F32),
                                            ALU.subtract).then_inc(glo_ok, 1)

                for s in range(2):
                    up_pair(0, s, UW, first=True)
                with dve.Fori(1, FT // 2 - 1) as j:
                    for s in range(2):
                        up_pair(j, s, UW)
                for s in range(2):
                    up_pair(FT // 2 - 1, s, DW)

                def down(m, e, cols):
                    if cols:
                        split(dn + m + 1, 0, cols)
                    dve.wait_ge(w_used, 2 * (dn + m) + 2)
                    xm = x[:, bass.ds(m, 1), :].rearrange("p o f -> p (o f)")
                    nc.vector.tensor_tensor(xm, ps[:, 4 + e, :], xm, ALU.add).then_inc(xe_ok, 1)
                    if cols:
                        split(dn + m + 1, 1, cols)
                    if not last_layer:
                        lo_tile(NORM_R, m, xm, h_hi[:, bass.ds(m, 1), :].rearrange("p o f -> p (o f)"),
                                h_lo[:, bass.ds(m, 1), :].rearrange("p o f -> p (o f)"),
                                gain[:, NORM_R, bass.ds(m, 1)])

                with dve.Fori(0, KT // 2 - 1) as j:
                    for e in range(2):
                        down(2 * j + e, e, DW)
                down(KT - 2, 0, DW)
                down(KT - 1, 1, 0 if last_layer else UW)

            mlp(0, False)

            def rotary(p, s, h, first=False):
                dve.wait_ge(w_used, 2 * p + s + 1)
                if first:
                    dve.wait_ge(csr_ok, 2)
                elif s == 0:
                    dve.wait_ge(xe_ok, XE_RO + KT * (h - 1))
                if s == 1:
                    dve.wait_ge(qlo_ok, 4 * h + 2)
                a, b = ps[:, 2 * s, :], ps[:, 2 * s + 1, :]
                nc.vector.tensor_tensor(rt[:, 0, :], a, csr[:, 0, :], ALU.mult)
                nc.vector.tensor_tensor(rt[:, 1, :], b, csr[:, 1, :], ALU.mult).then_inc(rt_ok, 1)
                nc.vector.tensor_tensor(rt[:, 2, :], b, csr[:, 0, :], ALU.mult)
                nc.vector.tensor_tensor(rt[:, 3, :], a, csr[:, 1, :], ALU.mult).then_inc(rt_ok, 1)

            def rotated_lo(h, s):
                for i in range(2):
                    n = 2 * s + i
                    dve.wait_ge(qhi_ok, 4 * h + n + 1)
                    nc.vector.tensor_tensor(qk_lo[:, n, :], rt[:, 2 * i, :], qk_hi[:, n, :].bitcast(F32),
                                            ALU.subtract).then_inc(qlo_ok, 1)

            def qkvg(h, first):
                p0 = PAIR_RET if first else PAIR_RET + 4 * h - 1
                pv = PAIR_RET + 1 if first else p0 + 2
                rotary(p0, 0, h, first)
                split(p0 + 1, 0, UW)
                rotated_lo(h, 0)
                rotary(p0, 1, h)
                split(p0 + 1, 1, UW)
                rotated_lo(h, 1)
                if not first:
                    dve.wait_ge(qlo_ok, 4 * h + 4)
                    for s in range(2):
                        project(h - 1, s, p0 + 1)
                        split(p0 + 2, s, UW)
                split(pv + 1, 0, UW)
                for t in range(PT):
                    dve.wait_ge(vhi_ok, 4 * h + t + 1)
                    nc.vector.scalar_tensor_tensor(v_lo[:, t, :], ps[:, 4 + t, :], rcol[:, 0, t:t + 1],
                                                   v_hi[:, t, :].bitcast(F32), ALU.mult,
                                                   ALU.subtract).then_inc(vlo_ok, 1)
                split(pv + 1, 1, UW)

                def p_lo_part(t):
                    dve.wait_ge(phi_ok, 4 * h + t + 1)
                    nc.vector.tensor_tensor(p_lo[:, t, 0:S - t * P], pf[:, t % 2, 0:S - t * P],
                                            p_hi[:, t, 0:S - t * P].bitcast(F32), ALU.subtract).then_inc(plo_ok, 1)

                for t in range(PT):
                    if t >= 2:
                        p_lo_part(t - 2)
                        dve.wait_ge(plo_ok, 4 * h + t - 1)
                    dve.wait_ge(rs_done, 4 * h + t + 1)
                    nc.vector.tensor_tensor(pf[:, t % 2, 0:S - t * P], ps[:, t, 0:S - t * P],
                                            dec[:, bass.ds(h, 1), 0:S - t * P].rearrange("p o f -> p (o f)"),
                                            ALU.mult).then_inc(pf_ok, 1)
                p_lo_part(2)
                p_lo_part(3)
                for s in range(2):
                    dve.wait_ge(w_used, 2 * (pv + 1) + s + 1)
                    for e in range(2):
                        m = 2 * s + e
                        nc.vector.tensor_tensor(sg[:, m, :], ps[:, 4 + m, :], rbc[:, 0, :],
                                                ALU.mult).then_inc(gx_ok, 1)
                    split(pv + 2, s, UW)

                def o_lo_part(m):
                    dve.wait_ge(ohi_ok, 4 * h + m + 1)
                    nc.vector.tensor_tensor(o_lo[:, m, :], sg[:, m, :], o_hi[:, m, :].bitcast(F32),
                                            ALU.subtract).then_inc(olo_ok, 1)

                for m in range(RV_T):
                    dve.wait_ge(o_done, 4 * h + m + 1)
                    dve.wait_ge(sg_ok, 4 * h + m + 1)
                    nc.vector.tensor_tensor(sg[:, m, :], ps[:, m, :], sg[:, m, :], ALU.mult).then_inc(ot_ok, 1)
                    if m > 0:
                        o_lo_part(m - 1)
                o_lo_part(RV_T - 1)
                variance(ST_HEAD + h, 1, R_V)

            def project(h, s, p):
                for e in range(4):
                    if e < 3:
                        dve.wait_ge(tile_done, TD_RO + 6 * h + 3 * s + e + 1)
                    else:
                        dve.wait_ge(w_used, 2 * p + s + 1)
                    if s == 0 and e == 0:
                        dve.wait_ge(bc_ok, BC_HEAD + h + 1)
                    if s == 1:
                        dve.wait_ge(xe_ok, XE_RO + KT * h + e + 1)
                    nc.vector.tensor_tensor(rt[:, e, :], ps[:, 4 + e, :], rbc[:, 1, :], ALU.mult).then_inc(pj_ok, 1)

            dve.wait_ge(r_in, 32)
            variance(ST_R, 0, D)
            qkvg(0, True)
            with dve.Fori(1, R_HEADS) as h:
                qkvg(h, False)
            for s in range(2):
                project(R_HEADS - 1, s, PAIR_UP[1] - 1)
                split(PAIR_UP[1], s, UW)
                for e in range(4):
                    lo_static(NORM_F1, 4 * s + e)

            mlp(1, True)

        @block.gpsimd
        def _(pool):
            steps = [0]

            def step(ins):
                steps[0] += 1
                ins.then_inc(pool_step, 1)
                pool.wait_ge(pool_step, steps[0])

            for dst, src in ((gqk[:, :, :], gain_qk), (rota[:, :, :, :], rot_a), (ident[:, :], ident_d),
                             (sink[:, :, :], sinks), (cvec[:, :, :, :], conv)):
                pool.dma_start(dst, src).then_inc(c_in, 16)
            nc.gpsimd.memset(ones[:, :], 1.0).then_inc(cst, 1)
            nc.gpsimd.memset(mhalf[:, :], -0.5).then_inc(cst, 1)
            pool.wait_ge(cst, 2)
            nc.gpsimd.memset(kTo[A_DH:P, 0, :, :, :], 0.0).then_inc(cst, 1)
            nc.gpsimd.memset(kTe[A_DH:P, 0, :, :, :], 0.0).then_inc(cst, 1)
            nc.gpsimd.memset(ve[CHUNK:P, 0, :], 0.0).then_inc(cst, 1)
            pool.wait_ge(cst, 5)
            nc.gpsimd.memset(kTo[0:A_DH, 1, :, :, :], 0.0).then_inc(cst, 1)
            nc.gpsimd.memset(kTe[0:A_DH, 1, :, :, :], 0.0).then_inc(cst, 1)
            pool.wait_ge(cst, 7)
            nc.gpsimd.memset(kTe[:, :, :, 0, CHUNK:P], 0.0).then_inc(cst, 1)
            pool.wait_ge(cst, 8)

            def add_square(base, m):
                if m == 0:
                    return
                pool.wait_ge(sq_ok, base + m + 1)
                if m == 1:
                    nc.gpsimd.tensor_tensor(ssum[:, :], sq[:, 0, :], sq[:, 1, :], ALU.add).then_inc(ssum_ok, 2)
                else:
                    pool.wait_ge(ssum_ok, base + m)
                    nc.gpsimd.tensor_tensor(ssum[:, :], ssum[:, :], sq[:, m % 2, :], ALU.add).then_inc(ssum_ok, 1)

            def add_squares(base, tiles):
                for m in range(tiles):
                    add_square(base, m)

            def inv_root(n, which):
                pool.wait_ge(var_ok, n + 1)
                nc.gpsimd.tensor_tensor(rcol[:, which, :], var[:, which, :], mhalf[:, 0:PT],
                                        ALU.pow).then_inc(r_ok, 1)

            add_squares(SQ_BASE[NORM_A], KT)
            inv_root(ST_A, 0)
            pool.wait_ge(c_in, 16 * 5)

            def q_root(n, heads):
                pool.wait_ge(qvar_ok, n + 1)
                nc.gpsimd.tensor_tensor(qs[:, n % 2, 0:heads], qvar[:, n % 2, 0:heads], mhalf[:, 0:heads],
                                        ALU.pow).then_inc(qs_ok, 1)

            def q_rotate(n, heads):
                t = n % PT
                v = kd[:, t, :, 0, :] if n < 4 else \
                    qn[:, t, (n - 4) // 4 * S:((n - 4) // 4 + 1) * S].rearrange("p (h d) -> p h d", d=A_DH)
                gi = 1 if n < 4 else 0
                half = A_ROT // 2
                pool.wait_ge(qn_ok, n + 1)
                step(nc.gpsimd.tensor_tensor(v, v, gqk[:, gi, :].unsqueeze(1).to_broadcast([P, heads, A_DH]), ALU.mult))
                nc.gpsimd.tensor_tensor(ra[:, 0:heads, :], v[:, :, 0:A_ROT],
                                        rota[:, 0, t, :].unsqueeze(1).to_broadcast([P, heads, A_ROT]), ALU.mult)
                nc.gpsimd.tensor_tensor(rb[:, 0:heads, 0:half], v[:, :, half:A_ROT],
                                        rota[:, 1, t, 0:half].unsqueeze(1).to_broadcast([P, heads, half]), ALU.mult)
                step(nc.gpsimd.tensor_tensor(rb[:, 0:heads, half:A_ROT], v[:, :, 0:half],
                                             rota[:, 1, t, half:A_ROT].unsqueeze(1).to_broadcast([P, heads, half]),
                                             ALU.mult))
                last = nc.gpsimd.tensor_tensor(v[:, :, 0:A_ROT], ra[:, 0:heads, :], rb[:, 0:heads, :], ALU.add)
                if n < 4:
                    step(last)
                    last = nc.gpsimd.tensor_copy(kd[:, t, :, 1, :], kd[:, t, :, 0, :])
                last.then_inc(qrot_ok, 1)

            def q_items(items, heads):
                for n in items:
                    q_root(n, heads)
                    q_rotate(n, heads)

            q_items(range(0, 4), 2)
            pool.wait_ge(v_ok, 4)
            pool.wait_ge(qrot_ok, 4)
            nc.gpsimd.tensor_copy(ve[0:CHUNK, :, :], va[0:CHUNK, :, :]).then_inc(ve_ok, 1)
            pool.wait_ge(ve_ok, 1)
            nc.gpsimd.tensor_copy(ve[CHUNK:P, 1:PT, :], va[CHUNK:P, 0:PT - 1, :]).then_inc(ve_ok, 1)
            pool.wait_ge(ve_ok, 2)
            q_items(range(4, 8), 8)
            q_items(range(8, 12), 8)

            for g, (c, n) in enumerate(GROUPS):
                r = g % 2
                nk = CHUNK if n == 0 else P
                if g >= 2:
                    pool.wait_ge(pt_done, g - 1)
                if g == 0:
                    pool.wait_ge(s_done, 1)
                if n == 0:
                    nc.gpsimd.memset(pn[:, r, :, CHUNK:P], 0.0).then_inc(pz_ok, 1)
                    pool.wait_ge(pz_ok, c + 1)
                pool.wait_ge(rd_ok, g + 1)
                nc.gpsimd.tensor_tensor(pn[:, r, :, 0:nk], ex[:, r, :, 0:nk],
                                        rd[:, r, :].unsqueeze(2).to_broadcast([P, 4, nk]), ALU.mult).then_inc(pn_ok, 1)

            add_squares(SQ_BASE[NORM_F0], KT)
            pool.wait_ge(w_used, 2 * PAIR_UP[0])
            nc.gpsimd.memset(u[:, :, 0:2], 0.0).then_inc(cst, 1)
            inv_root(ST_F0, 0)
            add_squares(SQ_BASE[NORM_R], KT)
            inv_root(ST_R, 0)

            pool.wait_ge(r_in, 32)
            pool.wait_ge(bc_ok, BC_R + 1)
            for i in range(2):
                nc.gpsimd.tensor_tensor(csr[:, i, :], tab[:, i, :], rbc[:, 0, :], ALU.mult).then_inc(csr_ok, 1)

            def qkvg(h, first):
                for s in range(2):
                    for i, op in ((0, ALU.subtract), (1, ALU.add)):
                        pool.wait_ge(rt_ok, 4 * h + 2 * s + i + 1)
                        nc.gpsimd.tensor_tensor(rt[:, 2 * i, :], rt[:, 2 * i, :], rt[:, 2 * i + 1, :],
                                                op).then_inc(rot_ok, 1)
                if not first:
                    for m in range(KT):
                        add_head(h - 1, m)
                add_squares(SQ_HEAD + 4 * h, RV_T)
                inv_root(ST_HEAD + h, 1)

            def add_head(h, m):
                pool.wait_ge(pj_ok, KT * h + m + 1)
                nc.gpsimd.tensor_tensor(x[:, m, :], x[:, m, :], rt[:, m % 4, :], ALU.add).then_inc(xe_ok, 1)

            qkvg(0, True)
            with pool.Fori(1, R_HEADS) as h:
                qkvg(h, False)
            for m in range(KT):
                add_head(R_HEADS - 1, m)
                if m > 0:
                    add_square(SQ_BASE[NORM_F1], m - 1)
            add_square(SQ_BASE[NORM_F1], KT - 1)
            pool.wait_ge(w_used, 2 * PAIR_UP[1])
            nc.gpsimd.memset(u[:, :, 0:2], 0.0).then_inc(cst, 1)
            inv_root(ST_F1, 0)

        @block.tensor
        def _(pe):
            def mm3(dst, st, mv, start, stop):
                nc.tensor.matmul(dst, st[0], mv[0], start=start, stop=False)
                nc.tensor.matmul(dst, st[0], mv[1], start=False, stop=False)
                return nc.tensor.matmul(dst, st[1], mv[0], start=False, stop=stop)

            def weights(s, c0, c1):
                return w_hi[:, s, c0:c1], w_lo[:, s, c0:c1]

            def hidden(k, c0=0, c1=S):
                return h_hi[:, k, c0:c1], h_lo[:, k, c0:c1]

            def unit(pair, s):
                pe.wait_ge(w_lo_ok, 2 * pair + s + 1)

            def columns(n, squares):
                pe.wait_ge(ssum_ok, squares)
                for t in range(PT):
                    last = nc.tensor.matmul(ps[:, 6, t:t + 1], ssum[:, t * P:(t + 1) * P], ones[:, :],
                                            start=True, stop=True)
                last.then_inc(col_done, 1)

            def broadcast(n, which):
                pe.wait_ge(r_ok, n + 1)
                for t in range(PT):
                    last = nc.tensor.matmul(ps[:, 7, t * P:(t + 1) * P],
                                            rcol[:, which, t:t + 1].to_broadcast([P, P]), ident[:, :],
                                            start=True, stop=True)
                last.then_inc(bc_done, 1)

            pe.wait_ge(cst, 1)
            for s in range(2):
                unit(PAIR_KV, s)
                for t in range(PT):
                    for k4 in range(4):
                        k = 4 * s + k4
                        if t == 0:
                            pe.wait_ge(h_ready, k + 1)
                        last = mm3(ps[:, t, 0:256], hidden(k, t * P, (t + 1) * P),
                                   weights(s, k4 * 256, (k4 + 1) * 256), k == 0, k == KT - 1)
                    if s == 1 and t < PT - 1:
                        last.then_inc(tile_done, 1)
                last.then_inc(w_used, 1)
            def turn_in(g):
                if g < 4:
                    pe.wait_ge(qn_ok, 4 + g + 1)
                elif g < 6:
                    pe.wait_ge(tp_ok, g - 3)
                elif g == 6:
                    pe.wait_ge(qn_ok, 10)
                else:
                    pe.wait_ge(tp_ok, g)
                pe.wait_ge(qrot_ok, 4 if g < 2 else (8 if g < 6 else 12))
                for t in range(PT):
                    src = kd[:, t, g, :, :].rearrange("p i d -> p (i d)") if g < 2 else \
                        qn[:, t, (g - 2) * P:(g - 1) * P]
                    last = nc.tensor.transpose(ps[:, turn_bank(g), t * P:(t + 1) * P], src, ident[:, :])
                last.then_inc(tp_done, 1)

            for cb in range(2):
                for s in range(2):
                    unit(PAIR_Q + cb, s)
                    for t in range(PT):
                        if cb == 0 and s == 0:
                            if t == 1:
                                columns(ST_A, SQ_BASE[NORM_A] + KT)
                            if t == 2:
                                pe.wait_ge(var_ok, ST_A + 1)
                        if cb == 1 and s == 0:
                            pe.wait_ge(v_ok, t + 1)
                            pe.wait_ge(qn_ok, t + 1)
                        for k4 in range(4):
                            k = 4 * s + k4
                            last = mm3(ps[:, (0 if cb else 4) + t, :], hidden(k, t * P, (t + 1) * P),
                                       weights(s, k4 * S, (k4 + 1) * S), k == 0, k == KT - 1)
                        if s == 1 and t < PT - 1:
                            last.then_inc(tile_done, 1)
                        if t == PT - 1:
                            last.then_inc(w_used, 1)
                        if cb == 1 and s == 1:
                            turn_in(2 + t)
                    if cb == 1 and s == 0:
                        pe.wait_ge(c_in, 16 * 5)
                        turn_in(0)
                        turn_in(1)

            def scores(g):
                c, n = GROUPS[g]
                if g == 0:
                    pe.wait_ge(tp_ok, 6)
                    pe.wait_ge(cst, 8)
                elif g == 2:
                    pe.wait_ge(qn_ok, 9)
                elif g >= 3:
                    pe.wait_ge(ex_ok, g - 2)
                if n == 0 and c == 1:
                    pe.wait_ge(tp_ok, 10)
                nk = CHUNK if n == 0 else P
                keys = kTe if n % 2 == 0 else kTo
                for i in range(4):
                    par, j = i // 2, 4 * c + 2 * (i % 2)
                    last = nc.tensor.matmul(ps[:, score_bank(g), i * P:i * P + nk],
                                            qT[:, n, j:j + 2, :].rearrange("p j q -> p (j q)"),
                                            keys[:, par, c, n // 2, 0:nk], start=True, stop=True)
                last.then_inc(s_done, 1)

            def turn(g):
                if g == 0:
                    pe.wait_ge(qn_ok, 12)
                else:
                    if g >= 2:
                        pe.wait_ge(pt_ok, g - 1)
                pe.wait_ge(pn_ok, g + 1)
                for i in range(4):
                    last = nc.tensor.transpose(ps[:, 2 + g % 2, i * P:(i + 1) * P], pn[:, g % 2, i, :], ident[:, :])
                last.then_inc(pt_done, 1)

            def values(g):
                c, n = GROUPS[g]
                pe.wait_ge(pt_ok, g + 1)
                if g == 0:
                    pe.wait_ge(ve_ok, 2)
                elif g >= 2:
                    pe.wait_ge(alo_ok, g - 1)
                v = ve if n % 2 == 0 else va
                for par in range(2):
                    last = nc.tensor.matmul(ps[par * A_DH:(par + 1) * A_DH, 4 + g % 2, 0:4 * CHUNK],
                                            v[:, n // 2, c * A_DH:(c + 1) * A_DH],
                                            pT[:, g % 2, par * 256:(par + 1) * 256], start=True, stop=True)
                last.then_inc(pv_done, 1)

            NG = len(GROUPS)
            for g in range(3):
                scores(g)
            for st in range(NG + 1):
                if st < NG:
                    turn(st)
                if st + 3 < NG:
                    scores(st + 3)
                if st < 4:
                    turn_in(6 + st)
                if st >= 1:
                    values(st - 1)

            for j in range(2):
                for s in range(2):
                    unit(PAIR_WO + j, s)
                    for e in range(2):
                        m = 4 * j + 2 * s + e
                        if m >= 4:
                            pe.wait_ge(xe_ok, XE_WO + m - 3)
                        for k in range(KT):
                            if m == 0 and k % 4 == 0:
                                pe.wait_ge(alo_ok, NCH * (k // 4 + 1))
                            last = mm3(ps[:, m % 4, :], weights(s, (e * KT + k) * P, (e * KT + k + 1) * P),
                                       (a_hi[:, k, :], a_lo[:, k, :]), k == 0, k == KT - 1)
                        last.then_inc(w_used if e else tile_done, 1)

            def mlp(layer):
                up, dn = PAIR_UP[layer], PAIR_DN[layer]
                norm = (NORM_F0, NORM_F1)[layer]

                def up_pair(j, s, first=False):
                    f = FT * layer + 2 * j + s
                    unit(up + j, s)
                    for ab in range(2):
                        if not first:
                            pe.wait_ge(u_ok, 2 * f - 3 + ab)
                        elif layer == 0:
                            pe.wait_ge(xe_ok, XE_WO + 5 + 2 * s + ab)
                        for k in range(KT):
                            if first and s == 0 and ab == 0:
                                pe.wait_ge(h_ready, KT * norm + k + 1)
                            c = (ab * KT + k) * P
                            last = mm3(ps[:, 2 * s + ab, :], weights(s, c, c + P), hidden(k), k == 0, k == KT - 1)
                        last.then_inc(w_used if ab else tile_done, 1)
                        if first and s == 0:
                            if ab == 0:
                                columns(ST_F1 if layer else ST_F0, SQ_BASE[norm] + KT)
                            else:
                                broadcast(ST_F1 if layer else ST_F0, 0)

                for s in range(2):
                    up_pair(0, s, first=True)
                with pe.Fori(1, FT // 2) as j:
                    for s in range(2):
                        up_pair(j, s)

                xe = (XE_DN0, XE_DN1)[layer]

                def down(m, e, wait_g=False):
                    if not (isinstance(m, int) and m < 2):
                        pe.wait_ge(xe_ok, xe + m - 1)
                    for s in range(2):
                        unit(dn + m, s)
                        for k11 in range(KH):
                            k = KH * s + k11
                            if wait_g and (k11 == 0 or k >= FT - 2):
                                pe.wait_ge(glo_ok, FT * layer + (KH if s == 0 else max(k + 1, FT - 2)))
                            last = mm3(ps[:, 4 + e, :], weights(s, k11 * P, (k11 + 1) * P),
                                       (g_hi[:, k, :], g_lo[:, k, :]), k == 0, k == FT - 1)
                        last.then_inc(w_used, 1)

                for e in range(2):
                    down(e, e, wait_g=(e == 0))
                with pe.Fori(1, KT // 2) as j:
                    for e in range(2):
                        down(2 * j + e, e)

            mlp(0)

            def qkvg(h, first):
                p0 = PAIR_RET if first else PAIR_RET + 4 * h - 1
                for s in range(2):
                    unit(p0, s)
                    for e in range(2):
                        if not first:
                            pe.wait_ge(sq_ok, SQ_HEAD + 4 * (h - 1) + 2 * s + e + 1)
                        for k in range(KT):
                            if first and s == 0 and e == 0:
                                pe.wait_ge(h_ready, KT * NORM_R + k + 1)
                            last = mm3(ps[:, 2 * s + e, :], weights(s, (e * KT + k) * P, (e * KT + k + 1) * P),
                                       hidden(k), k == 0, k == KT - 1)
                        if e == 1:
                            last.then_inc(w_used, 1)
                        if s == 0 and e == 0:
                            if first:
                                columns(ST_R, SQ_BASE[NORM_R] + KT)
                            else:
                                pe.wait_ge(gx_ok, 4 * h)
                                columns(ST_HEAD + h - 1, SQ_HEAD + 4 * h)
                        if s == 0 and e == 1:
                            if first:
                                broadcast(ST_R, 0)
                            else:
                                broadcast(ST_HEAD + h - 1, 1)
                if not first:
                    project(h - 1, p0 + 1)
                pv = PAIR_RET + 1 if first else p0 + 2
                for s in range(2):
                    unit(pv, s)
                    for t in range(PT):
                        if s == 0:
                            if not first:
                                pe.wait_ge(pj_ok, KT * (h - 1) + 5 + t)
                            elif t == 0:
                                pe.wait_ge(bc_ok, BC_R + 1)
                        for k4 in range(4):
                            k = 4 * s + k4
                            last = mm3(ps[:, 4 + t, :], hidden(k, t * P, (t + 1) * P),
                                       weights(s, k4 * S, (k4 + 1) * S), k == 0, k == KT - 1)
                    last.then_inc(w_used, 1)
                pe.wait_ge(qlo_ok, 4 * h + 4)
                for t in range(PT):
                    for d in range(2):
                        key, query = slice(t * P, (t + 1) * P), slice(t * P, S)
                        last = mm3(ps[:, t, 0:S - t * P], (qk_hi[:, 2 + d, key], qk_lo[:, 2 + d, key]),
                                   (qk_hi[:, d, query], qk_lo[:, d, query]), d == 0, d == 1)
                    last.then_inc(rs_done, 1)
                for s in range(2):
                    unit(pv + 1, s)
                    for e in range(2):
                        m = 2 * s + e
                        pe.wait_ge(vlo_ok, 4 * h + m + 1)
                        for k in range(KT):
                            last = mm3(ps[:, 4 + m, :], weights(s, (e * KT + k) * P, (e * KT + k + 1) * P),
                                       hidden(k), k == 0, k == KT - 1)
                    last.then_inc(w_used, 1)
                pe.wait_ge(plo_ok, 4 * h + 4)
                for m in range(RV_T):
                    for t in range(PT):
                        w = S - t * P
                        last = mm3(ps[:, m, t * P:S], (v_hi[:, t, m * P:(m + 1) * P], v_lo[:, t, m * P:(m + 1) * P]),
                                   (p_hi[:, t, 0:w], p_lo[:, t, 0:w]), t == 0, t == PT - 1)
                    last.then_inc(o_done, 1)

            def project(h, p, last_head=False):
                for s in range(2):
                    unit(p, s)
                    for e in range(4):
                        if last_head and s == 0 and e == 1:
                            columns(ST_HEAD + h, SQ_HEAD + 4 * (h + 1))
                        if last_head and s == 0 and e == 2:
                            pe.wait_ge(var_ok, ST_HEAD + h + 1)
                            broadcast(ST_HEAD + h, 1)
                        if s == 0 and e == 3:
                            pe.wait_ge(bc_ok, BC_HEAD + h + 1)
                        if s == 0:
                            pe.wait_ge(gx_ok, 4 * h + e + 1)
                        else:
                            pe.wait_ge(pj_ok, KT * h + e + 1)
                        for k in range(RV_T):
                            if s == 0 and e == 0:
                                pe.wait_ge(olo_ok, 4 * h + k + 1)
                            c = (e * RV_T + k) * P
                            last = mm3(ps[:, 4 + e, :], weights(s, c, c + P), (o_hi[:, k, :], o_lo[:, k, :]),
                                       k == 0, k == RV_T - 1)
                        last.then_inc(w_used if e == 3 else tile_done, 1)

            qkvg(0, True)
            with pe.Fori(1, R_HEADS) as h:
                qkvg(h, False)
            project(R_HEADS - 1, PAIR_UP[1] - 1, last_head=True)

            mlp(1)


def _tables():
    def angles(base, rot, half):
        inv = (np.float64(np.float32(base)) ** (-np.arange(half) * 2.0 / rot)).astype(np.float32)
        return (np.arange(S, dtype=np.float32)[:, None] * inv[None, :]).astype(np.float64)

    half = A_ROT // 2
    a = angles(ROPE_THETA, A_ROT, half)
    cos, sin = np.cos(a), np.sin(a)
    rot_a = np.stack([np.concatenate([cos, cos], 1), np.concatenate([-sin, sin], 1)])
    rot_a = rot_a.reshape(2, PT, P, A_ROT).transpose(2, 0, 1, 3).astype(np.float32)
    b = angles(R_BASE, R_QK, R_QK // 2)
    rot_r = np.stack([np.cos(b).T, np.sin(b).T], 1).astype(np.float32)
    lg = np.log1p(-np.power(2.0, -5.0 - np.arange(R_HEADS)))
    key, query = np.arange(P)[:, None, None], np.arange(S)[None, None, :]
    decay = np.exp(lg[None, :, None] * np.abs(query - key)) * (query // CHUNK >= key // CHUNK) * R_QK ** -0.5
    return np.eye(P, dtype=np.float32), rot_a, rot_r, decay.astype(np.float32)


def kernel(x, norm1_g, norm2_g, attn_w_qkv, attn_w_o, attn_q_gain, attn_k_gain, attn_sinks,
           ret_w_in, ret_w_o, ffn_w_up, ffn_conv_w, ffn_conv_b, ffn_w_down):
    import concourse.bacc as bacc
    from concourse.bass_utils import run_bass_kernel_spmd

    A = np.asarray
    c = np.ascontiguousarray
    arrays = {}
    arrays["xT"] = c(A(x)[0].T.reshape(KT, P, S))

    def moving(w, cols):
        return w.reshape(2, 4, P, cols).transpose(0, 2, 1, 3).reshape(2, P, 4 * cols)

    def stationary(w, kt, per):
        n = w.shape[1] // P
        return w.reshape(kt, P, n // per, per, P).transpose(2, 1, 3, 0, 4).reshape(n // per, P, per * kt * P)

    wqkv = A(attn_w_qkv)[0]
    arrays["w_kv"] = c(moving(wqkv[:, D:], 256))
    arrays["w_q"] = c(np.concatenate([moving(wqkv[:, 0:S], S), moving(wqkv[:, S:D], S)]))
    arrays["w_ao"] = c(stationary(A(attn_w_o)[0], KT, 2))
    for layer in range(2):
        wu = A(ffn_w_up)[layer].reshape(KT, P, 2, FT, P)
        wu_arr = c(wu.transpose(3, 1, 2, 0, 4).reshape(FT, P, UW))
        wd = A(ffn_w_down)[layer].reshape(2, KH, P, KT, P)
        wd_arr = c(wd.transpose(3, 0, 2, 1, 4).reshape(2 * KT, P, DW))
        arrays[f"w_up{layer}"], arrays[f"w_dn{layer}"] = wu_arr, wd_arr
    wr, wo = A(ret_w_in)[0], A(ret_w_o)[0]
    units = []
    for h in range(R_HEADS + 1):
        if h < R_HEADS:
            units += [stationary(wr[:, i * D + h * R_QK:i * D + (h + 1) * R_QK], KT, 2) for i in range(2)]
        if h > 0:
            units.append(stationary(wo[(h - 1) * R_V:h * R_V], RV_T, 4))
        if h < R_HEADS:
            units.append(moving(wr[:, 2 * D + h * R_V:2 * D + (h + 1) * R_V], R_V))
            units.append(stationary(wr[:, 4 * D + h * R_V:4 * D + (h + 1) * R_V], KT, 2))
    arrays["w_ret"] = c(np.concatenate(units))
    arrays["gains"] = c(np.stack([A(norm1_g)[0], A(norm2_g)[0], A(norm1_g)[1], A(norm2_g)[1]])
                        .reshape(4, KT, P).transpose(2, 0, 1))
    cw = np.concatenate([A(ffn_conv_w)[:, :, 0, :], A(ffn_conv_b)[:, None, :]], 1)
    arrays["conv"] = c(cw.reshape(2, 4, 2, FT, P).transpose(4, 0, 3, 2, 1).reshape(P, 2, FT, 8))
    arrays["gain_qk"] = c(np.broadcast_to(np.stack([A(attn_q_gain)[0], A(attn_k_gain)[0]])[None], (P, 2, A_DH)))
    sk = A(attn_sinks)[0].reshape(A_KVH, 2, 2, 2)
    sk = sk.transpose(2, 0, 3, 1).reshape(2, 1, A_KVH, 4)
    arrays["sinks"] = c(np.broadcast_to(sk, (2, CHUNK, A_KVH, 4)).reshape(P, A_KVH, 4))
    arrays["ident"], arrays["rot_a"], arrays["rot_r"], arrays["decay"] = (c(t) for t in _tables())

    nc = bacc.Bacc("TRN2", target_bir_lowering=False, num_devices=1)
    args = [nc.dram_tensor(f"in_{n}", a.shape, F32, kind="ExternalInput").ap() for n, a in arrays.items()]
    out = nc.dram_tensor("out", (KT, P, S), F32, kind="ExternalOutput").ap()
    names = list(arrays)
    by = dict(zip(names, args))
    trunk(nc, by["xT"], by["w_kv"], by["w_q"], by["w_ao"], by["w_up0"], by["w_dn0"], by["w_ret"], by["w_up1"],
          by["w_dn1"], by["gains"], by["conv"], by["gain_qk"], by["sinks"], by["ident"], by["rot_a"],
          by["rot_r"], by["decay"], out)
    r = run_bass_kernel_spmd(nc, [{f"in_{n}": a for n, a in arrays.items()}], core_ids=[0])
    got = r.results[0]["out"]
    return np.ascontiguousarray(got.reshape(D, S).T).reshape(1, S, D)
```

```python
from contextlib import ExitStack

import numpy as np

import concourse.bass as bass
from concourse import mybir

F32 = mybir.dt.float32
F32R = mybir.dt.float32r
ALU = mybir.AluOpType
ACT = mybir.ActivationFunctionType
AX = mybir.AxisListType

P = 128
D = 1024
S = 512
KT = D // P
PT = S // P
EPS = 1e-6
CHUNK = 64
NCH = S // CHUNK
A_DH, A_KVH = 64, 2
A_ROT = A_DH // 4
A_SCALE = A_DH ** -0.5
ROPE_THETA = 500000.0
R_HEADS = 4
R_QK = D // R_HEADS
R_V = 2 * D // R_HEADS
R_BASE = 10000.0
RV_T = R_V // P
D_FF = 2816
FT = D_FF // P
KH = FT // 2
UW = 2048
DW = KH * P
KVW = 4 * 256

PAIR_KV = 0
PAIR_Q = 1
PAIR_WO = 3
PAIR_UP = (5, 40)
PAIR_DN = (5 + FT // 2, 40 + FT // 2)
PAIR_RET = PAIR_DN[0] + KT
assert PAIR_RET == 24 and PAIR_RET + 4 * R_HEADS == PAIR_UP[1]

C_DMAS = 6
NORM_A, NORM_F0, NORM_R, NORM_F1 = range(4)
SQ_BASE = (0, KT, 2 * KT, 3 * KT + R_HEADS * RV_T)
SQ_HEAD = 3 * KT
XE_WO, XE_DN0 = 0, KT
XE_RO = 2 * KT
XE_DN1 = 2 * KT + R_HEADS * KT
TD_QKV = 0
TD_WO = 9
TD_UP0 = TD_WO + 4
TD_RO = TD_UP0 + FT
TD_UP1 = TD_RO + 6 * R_HEADS
ST_A, ST_F0, ST_R, ST_HEAD, ST_F1 = 0, 1, 2, 3, 3 + R_HEADS
BC_F0, BC_R, BC_HEAD, BC_F1 = 0, 1, 2, 2 + R_HEADS


def trunk(nc, xT, w_kv, w_q, w_ao, w_up0, w_dn0, w_ret, w_up1, w_dn1, gains, conv, gain_col, gain_rot, sinks,
          ident_d, rot_a, rot_r, decay, out):
    ctx = ExitStack()
    with ctx:
        def sb(name, shape, dt=F32, scope=ctx):
            return scope.enter_context(nc.sbuf_tensor(name, shape, dt))

        def sem(name):
            return ctx.enter_context(nc.semaphore(name))

        x = sb("x", [P, KT, S])
        h_hi = sb("h_hi", [P, KT, S], F32R)
        h_lo = sb("h_lo", [P, KT, S], F32R)
        raw = sb("raw", [P, 2, UW])
        w_hi = sb("w_hi", [P, 2, UW], F32R)
        w_lo = sb("w_lo", [P, 2, UW], F32R)
        gain = sb("gain", [P, 4, KT])
        cvec = sb("cvec", [P, 2, FT, 8])
        ident = sb("ident", [P, P])
        ones = sb("ones", [P, 1])
        warm = sb("warm", [P, 1])
        mhalf = sb("mhalf", [P, 8])
        sq = sb("sq", [P, 2, S])
        ssum = sb("ssum", [P, S])
        var = sb("var", [P, 2, PT])
        rcol = sb("rcol", [P, 2, PT])
        rbc = sb("rbc", [P, 2, S])
        ps = ctx.enter_context(nc.psum_tensor("ps", [P, 8, S], F32))

        att = ExitStack()
        qn = sb("qn", [P, PT, D], scope=att)
        kd = sb("kd", [P, PT, A_KVH, 2, A_DH], scope=att)
        va = sb("va", [P, PT, A_KVH * A_DH], scope=att)
        ve = sb("ve", [P, PT, A_KVH * A_DH], scope=att)
        qT = sb("qT", [P, NCH, KT, CHUNK], scope=att)
        kTo = sb("kTo", [P, 2, A_KVH, PT, P], scope=att)
        kTe = sb("kTe", [P, 2, A_KVH, PT, P], scope=att)
        a_hi = sb("a_hi", [P, KT, S], F32R, scope=att)
        a_lo = sb("a_lo", [P, KT, S], F32R, scope=att)
        sqq = sb("sqq", [P, 2, S], scope=att)
        qvar = sb("qvar", [P, 2, 8], scope=att)
        qss = sb("qss", [P, 2, 8], scope=att)
        qs = sb("qs", [P, 2, 8], scope=att)
        gcol = sb("gcol", [P, 2], scope=att)
        grot = sb("grot", [P, 2, 2, A_ROT], scope=att)
        rotg = sb("rotg", [P, 2, 2, PT, A_ROT], scope=att)
        rota = sb("rota", [P, 2, PT, A_ROT], scope=att)
        ra = sb("ra", [P, 8, A_ROT], scope=att)
        rb = sb("rb", [P, 8, A_ROT], scope=att)
        sink = sb("sink", [P, A_KVH, 4], scope=att)
        nsink = sb("nsink", [P, A_KVH, 4], scope=att)
        mx = sb("mx", [P, 2, 4], scope=att)
        nm = sb("nm", [P, 2, 4], scope=att)
        dm = sb("dm", [P, 2, 4], scope=att)
        es = sb("es", [P, 2, 4], scope=att)
        sm = sb("sm", [P, 2, 4], scope=att)
        den = sb("den", [P, 2, 4], scope=att)
        rd = sb("rd", [P, 2, 4], scope=att)
        ex = sb("ex", [P, 2, 4, P], scope=att)
        pn = qn[:, 0:2, 0:S].rearrange("p r (i k) -> p r i k", i=4)
        pT = qn[:, 2:4, 0:S]
        att.close()

        ffn = ExitStack()
        g_hi = sb("g_hi", [P, FT, S], F32R, scope=ffn)
        g_lo = sb("g_lo", [P, FT, S], F32R, scope=ffn)
        u = sb("u", [P, 2, S + 2], scope=ffn)
        y = sb("y", [P, 2, S], scope=ffn)
        gp = sb("gp", [P, S], scope=ffn)
        ffn.close()

        ret = ExitStack()
        rt = sb("rt", [P, 4, S], scope=ret)
        qk_hi = sb("qk_hi", [P, 4, S], F32R, scope=ret)
        qk_lo = sb("qk_lo", [P, 4, S], F32R, scope=ret)
        v_hi = sb("v_hi", [P, PT, R_V], F32R, scope=ret)
        v_lo = sb("v_lo", [P, PT, R_V], F32R, scope=ret)
        pf = sb("pf", [P, 2, S], scope=ret)
        p_hi = sb("p_hi", [P, PT, S], F32R, scope=ret)
        p_lo = sb("p_lo", [P, PT, S], F32R, scope=ret)
        sg = sb("sg", [P, RV_T, S], scope=ret)
        o_hi = sb("o_hi", [P, RV_T, S], F32R, scope=ret)
        o_lo = sb("o_lo", [P, RV_T, S], F32R, scope=ret)
        csr = sb("csr", [P, 2, S], scope=ret)
        dec = sb("dec", [P, R_HEADS, S], scope=ret)
        tab = rt[:, 0:2, :]
        ret.close()

        x_in = [sem(f"x_in{k}") for k in range(KT)]
        g_in = sem("g_in")
        c_in = sem("c_in")
        r_in = sem("r_in")
        o_out = sem("o_out")
        warm_ok = sem("warm_ok")
        w_half_ok = sem("w_half_ok")
        cst = sem("cst")
        w_loaded = [sem("w_loaded0"), sem("w_loaded1")]
        w_hi_ok, w_lo_ok, w_used = sem("w_hi_ok"), sem("w_lo_ok"), sem("w_used")
        tile_done = sem("tile_done")
        h_hi_ok, h_ready = sem("h_hi_ok"), sem("h_ready")
        sq_ok, ssum_ok = sem("sq_ok"), sem("ssum_ok")
        col_done, var_ok, r_ok, bc_done, bc_ok = (sem(n) for n in ("col_done", "var_ok", "r_ok", "bc_done", "bc_ok"))
        xe_ok = sem("xe_ok")
        v_ok, ve_ok = sem("v_ok"), sem("ve_ok")
        qsq_ok, qss_ok, qvar_ok, qs_ok, qn_ok, qrot_ok = (sem(n) for n in (
            "qsq_ok", "qss_ok", "qvar_ok", "qs_ok", "qn_ok", "qrot_ok"))
        pool_step = sem("pool_step")
        tp_done, tp_ok = sem("tp_done"), sem("tp_ok")
        s_done, mx_ok, nm_ok, dm_ok, ex_ok, den_ok, rd_ok, pn_ok = (sem(n) for n in (
            "s_done", "mx_ok", "nm_ok", "dm_ok", "ex_ok", "den_ok", "rd_ok", "pn_ok"))
        nsink_ok = sem("nsink_ok")
        pz_ok = sem("pz_ok")
        pt_done, pt_ok, pv_done, ahi_ok, alo_ok = (sem(n) for n in (
            "pt_done", "pt_ok", "pv_done", "ahi_ok", "alo_ok"))
        u_ok, yb_ok, y1_ok, y_ok, ge_ok, gp_ok, ghi_ok, glo_ok = (sem(n) for n in (
            "u_ok", "yb_ok", "y1_ok", "y_ok", "ge_ok", "gp_ok", "ghi_ok", "glo_ok"))
        csr_ok, rt_ok, rot_ok, qhi_ok, qlo_ok, vhi_ok, vlo_ok = (sem(n) for n in (
            "csr_ok", "rt_ok", "rot_ok", "qhi_ok", "qlo_ok", "vhi_ok", "vlo_ok"))
        rs_done, pf_ok, phi_ok, plo_ok, gx_ok, sg_ok = (sem(n) for n in (
            "rs_done", "pf_ok", "phi_ok", "plo_ok", "gx_ok", "sg_ok"))
        o_done, ot_ok, ohi_ok, olo_ok, pj_ok = (sem(n) for n in ("o_done", "ot_ok", "ohi_ok", "olo_ok", "pj_ok"))

        block = ctx.enter_context(nc.Block())

        def bank_of(n):
            return (n % PT) + (4 if 4 <= n < 8 else 0)

        def item_sums(eng, n):
            if n % PT < PT - 1:
                eng.wait_ge(tile_done, TD_QKV + 3 * (n // PT) + n % PT + 1)
            else:
                eng.wait_ge(w_used, 2 * (n // PT + 1))

        def score_bank(g):
            return (6, 7, 0)[g % 3]

        def turn_bank(g):
            return 3 - g if g < 2 else (4 + g % 4 if g < 6 else 3)

        def probs_bank(g):
            return 1 + g % 2

        GROUPS = [(g // NCH, g % NCH) for g in range(A_KVH * NCH)]

        @block.sync
        def _(sp):
            def load(src, pair, s, cols, first=False):
                if not first:
                    sp.wait_ge(w_lo_ok, 2 * pair + s - 1)
                sp.dma_start(raw[:, s, 0:cols], src).then_inc(w_loaded[s], 16)

            load(w_kv[0], PAIR_KV, 0, KVW, first=True)
            for k in range(KT):
                sp.dma_start(x[:, k, :], xT[k]).then_inc(x_in[k], 16)
                if k == 4:
                    load(w_kv[1], PAIR_KV, 1, KVW, first=True)
            for cb in range(2):
                for s in range(2):
                    load(w_q[2 * cb + s], PAIR_Q + cb, s, UW)
            for j in range(2):
                for s in range(2):
                    load(w_ao[2 * j + s], PAIR_WO + j, s, UW)

            def rows(src, i):
                return src[bass.ds(i, 1), :, :].rearrange("o p f -> (o p) f")

            def mlp(layer, w_up, w_dn):
                with sp.Fori(0, FT // 2) as j:
                    for s in range(2):
                        load(rows(w_up, 2 * j + s), PAIR_UP[layer] + j, s, UW)
                with sp.Fori(0, KT) as j:
                    for s in range(2):
                        load(rows(w_dn, 2 * j + s), PAIR_DN[layer] + j, s, DW)

            mlp(0, w_up0, w_dn0)
            with sp.Fori(0, 4 * R_HEADS) as j:
                for s in range(2):
                    load(rows(w_ret, 2 * j + s), PAIR_RET + j, s, UW)
            mlp(1, w_up1, w_dn1)
            for m in range(KT):
                sp.wait_ge(xe_ok, XE_DN1 + m + 1)
                sp.dma_start(out[m], x[:, m, :]).then_inc(o_out, 16)
            sp.wait_ge(o_out, 16 * KT)

        @block.scalar
        def _(act):
            act.dma_start(gain[:, :, :], gains).then_inc(g_in, 16)

            def split(pair, s, cols, first=False):
                act.wait_ge(w_loaded[s], 16 * (pair + 1))
                if not first:
                    act.wait_ge(w_used, 2 * pair + s - 1)
                nc.scalar.activation(w_hi[:, s, 0:cols], raw[:, s, 0:cols], ACT.Copy).then_inc(w_hi_ok, 1)

            def hi_part(norm, m):
                nc.scalar.activation(h_hi[:, m, :], x[:, m, :], ACT.Copy,
                                     scale=gain[:, norm, m:m + 1]).then_inc(h_hi_ok, 1)

            def hi_tile(norm, m):
                hi_part(norm, m)
                square(SQ_BASE[norm], m, x[:, m, :])

            def square(base, m, src):
                n = base + m
                if not (isinstance(n, int) and n < 2):
                    act.wait_ge(ssum_ok, n - 1)
                nc.scalar.activation(sq[:, m % 2, :], src, ACT.Square).then_inc(sq_ok, 1)

            def broadcast_out(n, which, bank=7):
                act.wait_ge(bc_done, n + 1)
                nc.scalar.activation(rbc[:, which, :], ps[:, bank, :], ACT.Copy).then_inc(bc_ok, 1)

            act.wait_ge(warm_ok, 1)
            nc.scalar.activation(warm[:, :], warm[:, :], ACT.Copy)
            act.wait_ge(w_loaded[0], 16)
            nc.scalar.activation(w_hi[:, 0, 0:KVW // 2], raw[:, 0, 0:KVW // 2], ACT.Copy).then_inc(w_half_ok, 1)
            nc.scalar.activation(w_hi[:, 0, KVW // 2:KVW], raw[:, 0, KVW // 2:KVW], ACT.Copy).then_inc(w_hi_ok, 1)
            act.wait_ge(g_in, 16)
            for k in range(KT):
                act.wait_ge(x_in[k], 16)
                hi_part(NORM_A, k)
                if k == 4:
                    split(PAIR_KV, 1, KVW, first=True)
            for k in range(KT):
                square(SQ_BASE[NORM_A], k, x[:, k, :])
                if k == 3:
                    split(PAIR_Q, 0, UW)
            split(PAIR_Q, 1, UW)

            def q_square(n, width):
                t = n % PT
                item_sums(act, n)
                if n >= 2:
                    act.wait_ge(qss_ok, n - 1)
                nc.scalar.activation(sqq[:, n % 2, 0:width], ps[:, bank_of(n), 0:width], ACT.Square,
                                     scale=rcol[:, 0, t:t + 1]).then_inc(qsq_ok, 1)

            def turned_out(g):
                act.wait_ge(tp_done, g + 1)
                b = ps[:, turn_bank(g), :]
                if g < 2:
                    own = b.rearrange("p (t c) -> p t c", c=P)
                    for par in range(2):
                        rows = slice(par * A_DH, (par + 1) * A_DH)
                        gk = gcol[rows, 1:2]
                        nc.scalar.activation(kTo[rows, par, g, :, :], own[rows], ACT.Copy, scale=gk)
                        nc.scalar.activation(kTe[rows, par, g, :, 0:CHUNK], own[rows, :, 0:CHUNK], ACT.Copy,
                                             scale=gk)
                        last = nc.scalar.activation(kTe[rows, par, g, 1:PT, CHUNK:P], own[rows, 0:PT - 1, CHUNK:P],
                                                    ACT.Copy, scale=gk)
                    last.then_inc(tp_ok, 1)
                else:
                    nc.scalar.activation(qT[:, :, g - 2, :], b.rearrange("p (n c) -> p n c", c=CHUNK),
                                         ACT.Copy, scale=gcol[:, 0:1]).then_inc(tp_ok, 1)

            act.wait_ge(r_ok, ST_A + 1)
            for t in range(PT):
                item_sums(act, t)
                nc.scalar.activation(va[:, t, :], ps[:, t, P:2 * P], ACT.Copy,
                                     scale=rcol[:, 0, t:t + 1]).then_inc(v_ok, 1)
                q_square(t, P)
            split(PAIR_Q + 1, 0, UW)
            act.wait_ge(c_in, 16 * C_DMAS)
            for n in range(4, 8):
                q_square(n, S)
                if n >= 6:
                    turned_out(n - 6)
            split(PAIR_Q + 1, 1, UW)
            def exps(g):
                _, n = GROUPS[g]
                nk = CHUNK if n == 0 else P
                r = g % 2
                act.wait_ge(dm_ok, g + 1)
                if g >= 2:
                    act.wait_ge(pn_ok, g - 1)
                for i in range(4):
                    nc.scalar.activation(ex[:, r, i, 0:nk], ps[:, score_bank(g), i * P:i * P + nk], ACT.Exp,
                                         scale=A_SCALE, bias=nm[:, r, i:i + 1], accum_out=sm[:, r, i:i + 1])
                nc.scalar.activation(es[:, r, :], dm[:, r, :], ACT.Exp).then_inc(ex_ok, 1)

            def probs_out(g):
                act.wait_ge(pt_done, g + 1)
                if g >= 2:
                    act.wait_ge(pv_done, g - 1)
                nc.scalar.activation(pT[:, g % 2, :], ps[:, probs_bank(g), :], ACT.Copy).then_inc(pt_ok, 1)

            split(PAIR_WO, 0, UW)
            q_square(8, S)
            for g in range(2, 6):
                turned_out(g)
            q_square(9, S)
            exps(0)
            q_square(10, S)
            exps(1)
            q_square(11, S)
            NG = len(GROUPS)
            for st in range(1, NG + 2):
                if 2 <= st < NG:
                    exps(st)
                if st >= 2:
                    probs_out(st - 2)
                if 3 <= st <= 6:
                    turned_out(3 + st)
            split(PAIR_WO, 1, UW)

            for j in range(2):
                for s in range(2):
                    for e in range(2):
                        m = 4 * j + 2 * s + e
                        act.wait_ge(xe_ok, XE_WO + m + 1)
                        hi_tile(NORM_F0, m)
                        if e == 0:
                            split(PAIR_WO + j + 1, s, UW)

            def mlp(layer, last_layer):
                up, dn = PAIR_UP[layer], PAIR_DN[layer]

                def up_pair(j, s, cols, first=False):
                    i = 2 * j + s
                    f = FT * layer + i
                    if first and s == 0:
                        broadcast_out(BC_F1 if layer else BC_F0, 0)
                    for ab in range(2):
                        act.wait_ge(u_ok, 2 * f + ab + 1)
                        c = cvec[:, layer, bass.ds(i, 1), 4 * ab + 2:4 * ab + 4].rearrange("p o f -> p (o f)")
                        nc.scalar.activation(y[:, ab, :], u[:, ab, 2:S + 2], ACT.Identity,
                                             scale=c[:, 0:1], bias=c[:, 1:2]).then_inc(yb_ok, 1)
                    split(up + j + 1, s, cols)
                    act.wait_ge(y_ok, 2 * f + 1)
                    nc.scalar.activation(y[:, 0, :], y[:, 0, :], ACT.Gelu).then_inc(ge_ok, 1)
                    act.wait_ge(gp_ok, f + 1)
                    nc.scalar.activation(g_hi[:, bass.ds(i, 1), :].rearrange("p o f -> p (o f)"), gp[:, :],
                                         ACT.Copy).then_inc(ghi_ok, 1)

                for s in range(2):
                    up_pair(0, s, UW, first=True)
                with act.Fori(1, FT // 2 - 1) as j:
                    for s in range(2):
                        up_pair(j, s, UW)
                for s in range(2):
                    up_pair(FT // 2 - 1, s, DW)

                def down(m, e, cols):
                    for s in range(2):
                        if cols:
                            split(dn + m + 1, s, cols)
                    if not last_layer:
                        act.wait_ge(ssum_ok, SQ_BASE[NORM_R] + m - 1)
                        act.wait_ge(xe_ok, XE_DN0 + m + 1)
                        gv = gain[:, NORM_R, bass.ds(m, 1)]
                        nc.scalar.activation(h_hi[:, bass.ds(m, 1), :].rearrange("p o f -> p (o f)"),
                                             x[:, bass.ds(m, 1), :].rearrange("p o f -> p (o f)"), ACT.Copy,
                                             scale=gv).then_inc(h_hi_ok, 1)
                        nc.scalar.activation(sq[:, e, :], x[:, bass.ds(m, 1), :].rearrange("p o f -> p (o f)"),
                                             ACT.Square).then_inc(sq_ok, 1)

                with act.Fori(0, KT // 2 - 1) as j:
                    for e in range(2):
                        down(2 * j + e, e, DW)
                down(KT - 2, 0, DW)
                down(KT - 1, 1, 0 if last_layer else UW)

            mlp(0, False)

            def qkvg(h, first):
                p0 = PAIR_RET if first else PAIR_RET + 4 * h - 1
                pv = PAIR_RET + 1 if first else p0 + 2
                split(p0 + 1, 0, UW)
                rotated(h, 0)
                if not first:
                    broadcast_out(BC_HEAD + h - 1, 1, bank=2)
                split(p0 + 1, 1, UW)
                rotated(h, 1)
                if not first:
                    for s in range(2):
                        split(p0 + 2, s, UW)
                split(pv + 1, 0, UW)
                act.wait_ge(w_used, 2 * pv + 2)
                for t in range(PT):
                    nc.scalar.activation(v_hi[:, t, :], ps[:, 4 + t, :], ACT.Copy,
                                         scale=rcol[:, 0, t:t + 1]).then_inc(vhi_ok, 1)
                split(pv + 1, 1, UW)
                for t in range(PT):
                    w = S - t * P
                    act.wait_ge(pf_ok, 4 * h + t + 1)
                    nc.scalar.activation(p_hi[:, t, 0:w], pf[:, t % 2, 0:w], ACT.Copy).then_inc(phi_ok, 1)
                for s in range(2):
                    for e in range(2):
                        m = 2 * s + e
                        act.wait_ge(gx_ok, 4 * h + m + 1)
                        nc.scalar.activation(sg[:, m, :], sg[:, m, :], ACT.Silu).then_inc(sg_ok, 1)
                    if s == 0:
                        split(pv + 2, 0, UW)
                for m in range(RV_T):
                    act.wait_ge(ot_ok, 4 * h + m + 1)
                    nc.scalar.activation(o_hi[:, m, :], sg[:, m, :], ACT.Copy).then_inc(ohi_ok, 1)
                    square(SQ_HEAD + 4 * h, m, ps[:, m, :])
                split(pv + 2, 1, UW)

            def rotated(h, s):
                for i in range(2):
                    act.wait_ge(rot_ok, 4 * h + 2 * s + i + 1)
                    nc.scalar.activation(qk_hi[:, 2 * s + i, :], rt[:, 2 * i, :], ACT.Copy).then_inc(qhi_ok, 1)

            act.wait_ge(w_used, 2 * PAIR_RET)
            act.dma_start(tab, rot_r).then_inc(r_in, 16)
            act.dma_start(dec[:, :, :], decay).then_inc(r_in, 16)
            broadcast_out(BC_R, 0)
            qkvg(0, True)
            with act.Fori(1, R_HEADS) as h:
                qkvg(h, False)
            broadcast_out(BC_HEAD + R_HEADS - 1, 1)
            for m in range(KT):
                act.wait_ge(xe_ok, XE_RO + KT * (R_HEADS - 1) + m + 1)
                hi_part(NORM_F1, m)
                for k in ((m,) if m < KT - 2 else (m - 1, m) if m == KT - 1 else ()):
                    square(SQ_BASE[NORM_F1], k, x[:, k, :])
                if m == 3:
                    split(PAIR_UP[1], 0, UW)
            split(PAIR_UP[1], 1, UW)

            mlp(1, True)

        @block.vector
        def _(dve):
            def split(pair, s, cols):
                dve.wait_ge(w_hi_ok, 2 * pair + s + 1)
                nc.vector.tensor_tensor(w_lo[:, s, 0:cols], raw[:, s, 0:cols], w_hi[:, s, 0:cols].bitcast(F32),
                                        ALU.subtract).then_inc(w_lo_ok, 1)

            def lo_tile(norm, m, xm, hm, lm, g):
                dve.wait_ge(h_hi_ok, KT * norm + m + 1)
                nc.vector.scalar_tensor_tensor(lm, xm, g, hm.bitcast(F32), ALU.mult,
                                               ALU.subtract).then_inc(h_ready, 1)

            def lo_static(norm, m):
                lo_tile(norm, m, x[:, m, :], h_hi[:, m, :], h_lo[:, m, :], gain[:, norm, m:m + 1])

            def variance(n, which, width, bank=6):
                dve.wait_ge(col_done, n + 1)
                nc.vector.tensor_scalar(var[:, which, :], ps[:, bank, 0:PT], 1.0 / width, EPS, ALU.mult,
                                        ALU.add).then_inc(var_ok, 1)

            def add_tile(m, bank):
                nc.vector.tensor_tensor(x[:, m, :], ps[:, bank, :], x[:, m, :], ALU.add).then_inc(xe_ok, 1)

            nc.vector.memset(warm[:, :], 0.0).then_inc(warm_ok, 1)
            dve.wait_ge(w_half_ok, 1)
            nc.vector.tensor_tensor(w_lo[:, 0, 0:KVW // 2], raw[:, 0, 0:KVW // 2],
                                    w_hi[:, 0, 0:KVW // 2].bitcast(F32), ALU.subtract)
            dve.wait_ge(w_hi_ok, 1)
            nc.vector.tensor_tensor(w_lo[:, 0, KVW // 2:KVW], raw[:, 0, KVW // 2:KVW],
                                    w_hi[:, 0, KVW // 2:KVW].bitcast(F32), ALU.subtract).then_inc(w_lo_ok, 1)
            for k in range(KT):
                lo_static(NORM_A, k)
                if k == 4:
                    split(PAIR_KV, 1, KVW)
            for m in range(1, KT):
                dve.wait_ge(sq_ok, SQ_BASE[NORM_A] + m + 1)
                if m == 1:
                    nc.vector.tensor_tensor(ssum[:, :], sq[:, 0, :], sq[:, 1, :], ALU.add).then_inc(ssum_ok, 2)
                else:
                    dve.wait_ge(ssum_ok, SQ_BASE[NORM_A] + m)
                    nc.vector.tensor_tensor(ssum[:, :], ssum[:, :], sq[:, m % 2, :], ALU.add).then_inc(ssum_ok, 1)
                if m == 3:
                    split(PAIR_Q, 0, UW)
            variance(ST_A, 0, D)
            split(PAIR_Q, 1, UW)

            def q_var(n, heads):
                dve.wait_ge(qsq_ok, n + 1)
                nc.vector.tensor_reduce(qss[:, n % 2, 0:heads],
                                        sqq[:, n % 2, 0:heads * A_DH].rearrange("p (h d) -> p h d", d=A_DH),
                                        AX.X, ALU.add).then_inc(qss_ok, 1)
                dve.wait_ge(qss_ok, n + 1)
                nc.vector.tensor_scalar(qvar[:, n % 2, 0:heads], qss[:, n % 2, 0:heads], 1.0 / A_DH, EPS,
                                        ALU.mult, ALU.add).then_inc(qvar_ok, 1)

            def q_norm(n, heads):
                t = n % PT
                src = ps[:, bank_of(n), 0:heads * A_DH].rearrange("p (h d) -> p h d", d=A_DH)
                if n < 4:
                    dst = kd[:, t, :, 0, :]
                else:
                    cb = (n - 4) // 4
                    dst = qn[:, t, cb * S:(cb + 1) * S].rearrange("p (h d) -> p h d", d=A_DH)
                dve.wait_ge(qs_ok, n + 1)
                nc.vector.scalar_tensor_tensor(dst, src, rcol[:, 0, t:t + 1],
                                               qs[:, n % 2, 0:heads].unsqueeze(2).to_broadcast([P, heads, A_DH]),
                                               ALU.mult, ALU.mult).then_inc(qn_ok, 1)

            def q_items(items, heads, pair, s, after):
                q_var(items[0], heads)
                for n in items:
                    if n + 1 in items:
                        q_var(n + 1, heads)
                    q_norm(n, heads)
                    if n == after:
                        split(pair, s, UW)

            q_items(range(0, 4), 2, PAIR_Q + 1, 0, after=3)
            q_items(range(4, 8), 8, PAIR_Q + 1, 1, after=5)
            dve.wait_ge(c_in, 16 * C_DMAS)
            nc.vector.tensor_scalar(nsink[:, :, :], sink[:, :, :], -1.0, None, ALU.mult).then_inc(nsink_ok, 1)
            dve.wait_ge(nsink_ok, 1)

            def softmax_top(g):
                c, n = GROUPS[g]
                nk = CHUNK if n == 0 else P
                r = g % 2
                dve.wait_ge(s_done, g + 1)
                nc.vector.tensor_reduce(mx[:, r, :],
                                        ps[:, score_bank(g), :].rearrange("p (i k) -> p i k", k=P)[:, :, 0:nk],
                                        AX.X, ALU.max).then_inc(mx_ok, 1)
                dve.wait_ge(mx_ok, g + 1)
                nc.vector.scalar_tensor_tensor(nm[:, r, :], mx[:, r, :], -A_SCALE, nsink[:, c, :], ALU.mult,
                                               ALU.min).then_inc(nm_ok, 1)
                dve.wait_ge(nm_ok, g + 1)
                nc.vector.tensor_tensor(dm[:, r, :], sink[:, c, :], nm[:, r, :], ALU.add).then_inc(dm_ok, 1)

            def softmax_bottom(g):
                r = g % 2
                dve.wait_ge(ex_ok, g + 1)
                nc.vector.tensor_tensor(den[:, r, :], sm[:, r, :], es[:, r, :], ALU.add).then_inc(den_ok, 1)
                dve.wait_ge(den_ok, g + 1)
                nc.vector.reciprocal(rd[:, r, :], den[:, r, :]).then_inc(rd_ok, 1)

            def heads_out(g):
                c, n = GROUPS[g]
                src = ps[:, 4 + g % 2, 0:4 * CHUNK].rearrange("p (j q) -> p j q", q=CHUNK)
                dst = (slice(None), slice(4 * c, 4 * c + 4), slice(n * CHUNK, (n + 1) * CHUNK))
                dve.wait_ge(pv_done, g + 1)
                nc.vector.tensor_copy(a_hi[dst], src).then_inc(ahi_ok, 1)
                dve.wait_ge(ahi_ok, g + 1)
                nc.vector.tensor_tensor(a_lo[dst], src, a_hi[dst].bitcast(F32), ALU.subtract).then_inc(alo_ok, 1)

            split(PAIR_WO, 0, UW)

            q_var(8, 8)
            q_norm(8, 8)
            q_var(9, 8)
            softmax_top(0)
            q_norm(9, 8)
            softmax_bottom(0)
            q_var(10, 8)
            softmax_top(1)
            softmax_bottom(1)
            q_norm(10, 8)
            softmax_top(2)
            q_var(11, 8)
            NG = len(GROUPS)
            for st in range(2, NG + 3):
                if st + 1 < NG:
                    softmax_top(st + 1)
                if st < NG:
                    softmax_bottom(st)
                if st == 2:
                    q_norm(11, 8)
                if st >= 3:
                    heads_out(st - 3)
            split(PAIR_WO, 1, UW)

            for j in range(2):
                for s in range(2):
                    for e in range(2):
                        m = 4 * j + 2 * s + e
                        if e == 0:
                            dve.wait_ge(tile_done, TD_WO + 2 * j + s + 1)
                        else:
                            dve.wait_ge(w_used, 2 * (PAIR_WO + j) + s + 1)
                        add_tile(m, m % 4)
                        if m > 0:
                            lo_static(NORM_F0, m - 1)
                        if e == 1:
                            split(PAIR_WO + j + 1, s, UW)
            lo_static(NORM_F0, KT - 1)

            def mlp(layer, last_layer):
                up, dn = PAIR_UP[layer], PAIR_DN[layer]
                td = (TD_UP0, TD_UP1)[layer]

                def up_pair(j, s, cols, first=False):
                    i = 2 * j + s
                    f = FT * layer + i
                    c = cvec[:, layer, bass.ds(i, 1), :].rearrange("p o f -> p (o f)")
                    if first and s == 0:
                        variance(ST_F1 if layer else ST_F0, 0, D)
                        dve.wait_ge(cst, 9 + layer)
                        dve.wait_ge(bc_ok, (BC_F1 if layer else BC_F0) + 1)
                    dve.wait_ge(tile_done, td + i + 1)
                    nc.vector.tensor_tensor(u[:, 0, 2:S + 2], ps[:, 2 * s, :], rbc[:, 0, :], ALU.mult).then_inc(u_ok, 1)
                    dve.wait_ge(w_used, 2 * (up + j) + s + 1)
                    nc.vector.tensor_tensor(u[:, 1, 2:S + 2], ps[:, 2 * s + 1, :], rbc[:, 0, :],
                                            ALU.mult).then_inc(u_ok, 1)
                    for ab in range(2):
                        dve.wait_ge(yb_ok, 2 * f + ab + 1)
                        nc.vector.scalar_tensor_tensor(y[:, ab, :], u[:, ab, 1:S + 1], c[:, 4 * ab + 1:4 * ab + 2],
                                                       y[:, ab, :], ALU.mult, ALU.add).then_inc(y1_ok, 1)
                    for ab in range(2):
                        dve.wait_ge(y1_ok, 2 * f + ab + 1)
                        nc.vector.scalar_tensor_tensor(y[:, ab, :], u[:, ab, 0:S], c[:, 4 * ab:4 * ab + 1],
                                                       y[:, ab, :], ALU.mult, ALU.add).then_inc(y_ok, 1)
                    split(up + j + 1, s, cols)
                    dve.wait_ge(ge_ok, f + 1)
                    dve.wait_ge(y_ok, 2 * f + 2)
                    nc.vector.tensor_tensor(gp[:, :], y[:, 0, :], y[:, 1, :], ALU.mult).then_inc(gp_ok, 1)
                    dve.wait_ge(ghi_ok, f + 1)
                    gi = (slice(None), bass.ds(i, 1), slice(None))
                    nc.vector.tensor_tensor(g_lo[gi].rearrange("p o f -> p (o f)"), gp[:, :],
                                            g_hi[gi].rearrange("p o f -> p (o f)").bitcast(F32),
                                            ALU.subtract).then_inc(glo_ok, 1)

                for s in range(2):
                    up_pair(0, s, UW, first=True)
                with dve.Fori(1, FT // 2 - 1) as j:
                    for s in range(2):
                        up_pair(j, s, UW)
                for s in range(2):
                    up_pair(FT // 2 - 1, s, DW)

                def down(m, e, cols):
                    if cols:
                        split(dn + m + 1, 0, cols)
                    dve.wait_ge(w_used, 2 * (dn + m) + 2)
                    xm = x[:, bass.ds(m, 1), :].rearrange("p o f -> p (o f)")
                    nc.vector.tensor_tensor(xm, ps[:, 4 + e, :], xm, ALU.add).then_inc(xe_ok, 1)
                    if cols:
                        split(dn + m + 1, 1, cols)
                    if not last_layer:
                        lo_tile(NORM_R, m, xm, h_hi[:, bass.ds(m, 1), :].rearrange("p o f -> p (o f)"),
                                h_lo[:, bass.ds(m, 1), :].rearrange("p o f -> p (o f)"),
                                gain[:, NORM_R, bass.ds(m, 1)])

                with dve.Fori(0, KT // 2 - 1) as j:
                    for e in range(2):
                        down(2 * j + e, e, DW)
                down(KT - 2, 0, DW)
                down(KT - 1, 1, 0 if last_layer else UW)

            mlp(0, False)

            def rotary(p, s, h, first=False):
                dve.wait_ge(w_used, 2 * p + s + 1)
                if first:
                    dve.wait_ge(csr_ok, 2)
                elif s == 0:
                    dve.wait_ge(xe_ok, XE_RO + KT * (h - 1))
                if s == 1:
                    dve.wait_ge(qlo_ok, 4 * h + 2)
                a, b = ps[:, 4 + 2 * s, :], ps[:, 5 + 2 * s, :]
                nc.vector.tensor_tensor(rt[:, 0, :], a, csr[:, 0, :], ALU.mult)
                nc.vector.tensor_tensor(rt[:, 1, :], b, csr[:, 1, :], ALU.mult).then_inc(rt_ok, 1)
                nc.vector.tensor_tensor(rt[:, 2, :], b, csr[:, 0, :], ALU.mult)
                nc.vector.tensor_tensor(rt[:, 3, :], a, csr[:, 1, :], ALU.mult).then_inc(rt_ok, 1)

            def rotated_lo(h, s):
                for i in range(2):
                    n = 2 * s + i
                    dve.wait_ge(qhi_ok, 4 * h + n + 1)
                    nc.vector.tensor_tensor(qk_lo[:, n, :], rt[:, 2 * i, :], qk_hi[:, n, :].bitcast(F32),
                                            ALU.subtract).then_inc(qlo_ok, 1)

            def qkvg(h, first):
                p0 = PAIR_RET if first else PAIR_RET + 4 * h - 1
                pv = PAIR_RET + 1 if first else p0 + 2
                rotary(p0, 0, h, first)
                split(p0 + 1, 0, UW)
                rotated_lo(h, 0)
                rotary(p0, 1, h)
                split(p0 + 1, 1, UW)
                rotated_lo(h, 1)
                if not first:
                    dve.wait_ge(qlo_ok, 4 * h + 4)
                    for s in range(2):
                        for e in range(4):
                            project(h - 1, s, e, p0 + 1)
                        split(p0 + 2, s, UW)
                split(pv + 1, 0, UW)
                for t in range(PT):
                    dve.wait_ge(vhi_ok, 4 * h + t + 1)
                    nc.vector.scalar_tensor_tensor(v_lo[:, t, :], ps[:, 4 + t, :], rcol[:, 0, t:t + 1],
                                                   v_hi[:, t, :].bitcast(F32), ALU.mult,
                                                   ALU.subtract).then_inc(vlo_ok, 1)
                split(pv + 1, 1, UW)

                def p_lo_part(t):
                    dve.wait_ge(phi_ok, 4 * h + t + 1)
                    nc.vector.tensor_tensor(p_lo[:, t, 0:S - t * P], pf[:, t % 2, 0:S - t * P],
                                            p_hi[:, t, 0:S - t * P].bitcast(F32), ALU.subtract).then_inc(plo_ok, 1)

                for t in range(PT):
                    if t >= 2:
                        p_lo_part(t - 2)
                        dve.wait_ge(plo_ok, 4 * h + t - 1)
                    dve.wait_ge(rs_done, 4 * h + t + 1)
                    nc.vector.tensor_tensor(pf[:, t % 2, 0:S - t * P], ps[:, t, 0:S - t * P],
                                            dec[:, bass.ds(h, 1), 0:S - t * P].rearrange("p o f -> p (o f)"),
                                            ALU.mult).then_inc(pf_ok, 1)
                p_lo_part(2)
                p_lo_part(3)
                for s in range(2):
                    dve.wait_ge(w_used, 2 * (pv + 1) + s + 1)
                    for e in range(2):
                        m = 2 * s + e
                        nc.vector.tensor_tensor(sg[:, m, :], ps[:, 4 + m, :], rbc[:, 0, :],
                                                ALU.mult).then_inc(gx_ok, 1)
                    if s == 0:
                        split(pv + 2, 0, UW)

                def o_lo_part(m):
                    dve.wait_ge(ohi_ok, 4 * h + m + 1)
                    nc.vector.tensor_tensor(o_lo[:, m, :], sg[:, m, :], o_hi[:, m, :].bitcast(F32),
                                            ALU.subtract).then_inc(olo_ok, 1)

                for m in range(RV_T):
                    dve.wait_ge(o_done, 4 * h + m + 1)
                    dve.wait_ge(sg_ok, 4 * h + m + 1)
                    nc.vector.tensor_tensor(sg[:, m, :], ps[:, m, :], sg[:, m, :], ALU.mult).then_inc(ot_ok, 1)
                    if m > 0:
                        o_lo_part(m - 1)
                o_lo_part(RV_T - 1)
                split(pv + 2, 1, UW)
                variance(ST_HEAD + h, 1, R_V, bank=3)

            def project(h, s, e, p):
                if e < 3:
                    dve.wait_ge(tile_done, TD_RO + 6 * h + 3 * s + e + 1)
                else:
                    dve.wait_ge(w_used, 2 * p + s + 1)
                if s == 0 and e == 0:
                    dve.wait_ge(bc_ok, BC_HEAD + h + 1)
                if s == 1:
                    dve.wait_ge(xe_ok, XE_RO + KT * h + e + 1)
                nc.vector.tensor_tensor(rt[:, e, :], ps[:, e, :], rbc[:, 1, :], ALU.mult).then_inc(pj_ok, 1)

            dve.wait_ge(r_in, 32)
            variance(ST_R, 0, D)
            qkvg(0, True)
            with dve.Fori(1, R_HEADS) as h:
                qkvg(h, False)
            for m in range(KT):
                project(R_HEADS - 1, m // 4, m % 4, PAIR_UP[1] - 1)
                if m >= 2:
                    lo_static(NORM_F1, m - 2)
                if m == 4:
                    split(PAIR_UP[1], 0, UW)
            lo_static(NORM_F1, KT - 2)
            lo_static(NORM_F1, KT - 1)
            split(PAIR_UP[1], 1, UW)

            mlp(1, True)

        @block.gpsimd
        def _(pool):
            steps = [0]

            def step(ins):
                steps[0] += 1
                ins.then_inc(pool_step, 1)
                pool.wait_ge(pool_step, steps[0])

            for dst, src in ((gcol[:, :], gain_col), (grot[:, :, :, :], gain_rot), (rota[:, :, :, :], rot_a),
                             (ident[:, :], ident_d),
                             (sink[:, :, :], sinks), (cvec[:, :, :, :], conv)):
                pool.dma_start(dst, src).then_inc(c_in, 16)
            nc.gpsimd.memset(ones[:, :], 1.0).then_inc(cst, 1)
            nc.gpsimd.memset(mhalf[:, :], -0.5).then_inc(cst, 1)
            pool.wait_ge(cst, 2)
            nc.gpsimd.memset(kTo[A_DH:P, 0, :, :, :], 0.0).then_inc(cst, 1)
            nc.gpsimd.memset(kTe[A_DH:P, 0, :, :, :], 0.0).then_inc(cst, 1)
            nc.gpsimd.memset(ve[CHUNK:P, 0, :], 0.0).then_inc(cst, 1)
            pool.wait_ge(cst, 5)
            nc.gpsimd.memset(kTo[0:A_DH, 1, :, :, :], 0.0).then_inc(cst, 1)
            nc.gpsimd.memset(kTe[0:A_DH, 1, :, :, :], 0.0).then_inc(cst, 1)
            pool.wait_ge(cst, 7)
            nc.gpsimd.memset(kTe[:, :, :, 0, CHUNK:P], 0.0).then_inc(cst, 1)
            pool.wait_ge(cst, 8)

            def add_square(base, m):
                if m == 0:
                    return
                pool.wait_ge(sq_ok, base + m + 1)
                if m == 1:
                    nc.gpsimd.tensor_tensor(ssum[:, :], sq[:, 0, :], sq[:, 1, :], ALU.add).then_inc(ssum_ok, 2)
                else:
                    pool.wait_ge(ssum_ok, base + m)
                    nc.gpsimd.tensor_tensor(ssum[:, :], ssum[:, :], sq[:, m % 2, :], ALU.add).then_inc(ssum_ok, 1)

            def add_squares(base, tiles):
                for m in range(tiles):
                    add_square(base, m)

            def inv_root(n, which):
                pool.wait_ge(var_ok, n + 1)
                nc.gpsimd.tensor_tensor(rcol[:, which, :], var[:, which, :], mhalf[:, 0:PT],
                                        ALU.pow).then_inc(r_ok, 1)

            pool.wait_ge(c_in, 16 * C_DMAS)
            for i in range(2):
                for cs in range(2):
                    last = nc.gpsimd.tensor_tensor(rotg[:, i, cs, :, :], rota[:, cs, :, :],
                                                   grot[:, i, cs, :].unsqueeze(1).to_broadcast([P, PT, A_ROT]),
                                                   ALU.mult)
            step(last)
            inv_root(ST_A, 0)

            def q_root(n, heads):
                pool.wait_ge(qvar_ok, n + 1)
                nc.gpsimd.tensor_tensor(qs[:, n % 2, 0:heads], qvar[:, n % 2, 0:heads], mhalf[:, 0:heads],
                                        ALU.pow).then_inc(qs_ok, 1)

            def q_rotate(n, heads):
                t = n % PT
                v = kd[:, t, :, 0, :] if n < 4 else \
                    qn[:, t, (n - 4) // 4 * S:((n - 4) // 4 + 1) * S].rearrange("p (h d) -> p h d", d=A_DH)
                tb = rotg[:, 1 if n < 4 else 0, :, t, :]
                half = A_ROT // 2
                pool.wait_ge(qn_ok, n + 1)
                if n > 0:
                    pool.wait_ge(qrot_ok, n)
                nc.gpsimd.tensor_tensor(ra[:, 0:heads, :], v[:, :, 0:A_ROT],
                                        tb[:, 0, :].unsqueeze(1).to_broadcast([P, heads, A_ROT]), ALU.mult)
                nc.gpsimd.tensor_tensor(rb[:, 0:heads, 0:half], v[:, :, half:A_ROT],
                                        tb[:, 1, 0:half].unsqueeze(1).to_broadcast([P, heads, half]), ALU.mult)
                step(nc.gpsimd.tensor_tensor(rb[:, 0:heads, half:A_ROT], v[:, :, 0:half],
                                             tb[:, 1, half:A_ROT].unsqueeze(1).to_broadcast([P, heads, half]),
                                             ALU.mult))
                last = nc.gpsimd.tensor_tensor(v[:, :, 0:A_ROT], ra[:, 0:heads, :], rb[:, 0:heads, :], ALU.add)
                if n < 4:
                    step(last)
                    last = nc.gpsimd.tensor_copy(kd[:, t, :, 1, :], kd[:, t, :, 0, :])
                last.then_inc(qrot_ok, 1)

            def q_items(items, heads):
                q_root(items[0], heads)
                for n in items:
                    if n + 1 in items:
                        q_root(n + 1, heads)
                    q_rotate(n, heads)

            q_items(range(0, 4), 2)
            pool.wait_ge(v_ok, 4)
            pool.wait_ge(qrot_ok, 4)
            nc.gpsimd.tensor_copy(ve[0:CHUNK, :, :], va[0:CHUNK, :, :]).then_inc(ve_ok, 1)
            pool.wait_ge(ve_ok, 1)
            nc.gpsimd.tensor_copy(ve[CHUNK:P, 1:PT, :], va[CHUNK:P, 0:PT - 1, :]).then_inc(ve_ok, 1)
            pool.wait_ge(ve_ok, 2)
            q_items(range(4, 8), 8)

            def probs(g):
                c, n = GROUPS[g]
                r = g % 2
                nk = CHUNK if n == 0 else P
                if g >= 2:
                    pool.wait_ge(pt_done, g - 1)
                if g == 0:
                    pool.wait_ge(s_done, 1)
                if n == 0:
                    nc.gpsimd.memset(pn[:, r, :, CHUNK:P], 0.0).then_inc(pz_ok, 1)
                    pool.wait_ge(pz_ok, c + 1)
                pool.wait_ge(rd_ok, g + 1)
                nc.gpsimd.tensor_tensor(pn[:, r, :, 0:nk], ex[:, r, :, 0:nk],
                                        rd[:, r, :].unsqueeze(2).to_broadcast([P, 4, nk]), ALU.mult).then_inc(pn_ok, 1)

            q_root(8, 8)
            q_rotate(8, 8)
            q_root(9, 8)
            q_rotate(9, 8)
            probs(0)
            q_root(10, 8)
            probs(1)
            q_rotate(10, 8)
            q_root(11, 8)
            probs(2)
            q_rotate(11, 8)
            for g in range(3, len(GROUPS)):
                probs(g)

            add_squares(SQ_BASE[NORM_F0], KT)
            pool.wait_ge(w_used, 2 * PAIR_UP[0])
            nc.gpsimd.memset(u[:, :, 0:2], 0.0).then_inc(cst, 1)
            inv_root(ST_F0, 0)
            add_squares(SQ_BASE[NORM_R], KT)
            inv_root(ST_R, 0)

            pool.wait_ge(r_in, 32)
            pool.wait_ge(bc_ok, BC_R + 1)
            for i in range(2):
                nc.gpsimd.tensor_tensor(csr[:, i, :], tab[:, i, :], rbc[:, 0, :], ALU.mult).then_inc(csr_ok, 1)

            def qkvg(h, first):
                for s in range(2):
                    for i, op in ((0, ALU.subtract), (1, ALU.add)):
                        pool.wait_ge(rt_ok, 4 * h + 2 * s + i + 1)
                        nc.gpsimd.tensor_tensor(rt[:, 2 * i, :], rt[:, 2 * i, :], rt[:, 2 * i + 1, :],
                                                op).then_inc(rot_ok, 1)
                if not first:
                    for m in range(KT):
                        add_head(h - 1, m)
                add_squares(SQ_HEAD + 4 * h, RV_T)
                inv_root(ST_HEAD + h, 1)

            def add_head(h, m):
                pool.wait_ge(pj_ok, KT * h + m + 1)
                nc.gpsimd.tensor_tensor(x[:, m, :], x[:, m, :], rt[:, m % 4, :], ALU.add).then_inc(xe_ok, 1)

            qkvg(0, True)
            with pool.Fori(1, R_HEADS) as h:
                qkvg(h, False)
            for m in range(KT):
                add_head(R_HEADS - 1, m)
                if 0 < m < KT - 2:
                    add_square(SQ_BASE[NORM_F1], m - 1)
            for m in range(KT - 3, KT):
                add_square(SQ_BASE[NORM_F1], m)
            pool.wait_ge(w_used, 2 * PAIR_UP[1])
            nc.gpsimd.memset(u[:, :, 0:2], 0.0).then_inc(cst, 1)
            inv_root(ST_F1, 0)

        @block.tensor
        def _(pe):
            def mm3(dst, st, mv, start, stop):
                nc.tensor.matmul(dst, st[0], mv[0], start=start, stop=False)
                nc.tensor.matmul(dst, st[0], mv[1], start=False, stop=False)
                return nc.tensor.matmul(dst, st[1], mv[0], start=False, stop=stop)

            def weights(s, c0, c1):
                return w_hi[:, s, c0:c1], w_lo[:, s, c0:c1]

            def hidden(k, c0=0, c1=S):
                return h_hi[:, k, c0:c1], h_lo[:, k, c0:c1]

            def unit(pair, s):
                pe.wait_ge(w_lo_ok, 2 * pair + s + 1)

            def columns(n, squares, bank=6):
                pe.wait_ge(ssum_ok, squares)
                for t in range(PT):
                    last = nc.tensor.matmul(ps[:, bank, t:t + 1], ssum[:, t * P:(t + 1) * P], ones[:, :],
                                            start=True, stop=True)
                last.then_inc(col_done, 1)

            def broadcast(n, which, bank=7):
                pe.wait_ge(r_ok, n + 1)
                for t in range(PT):
                    last = nc.tensor.matmul(ps[:, bank, t * P:(t + 1) * P],
                                            rcol[:, which, t:t + 1].to_broadcast([P, P]), ident[:, :],
                                            start=True, stop=True)
                last.then_inc(bc_done, 1)

            pe.wait_ge(cst, 1)
            for s in range(2):
                unit(PAIR_KV, s)
                for t in range(PT):
                    for k4 in range(4):
                        k = 4 * s + k4
                        if t == 0:
                            pe.wait_ge(h_ready, k + 1)
                        last = mm3(ps[:, t, 0:256], hidden(k, t * P, (t + 1) * P),
                                   weights(s, k4 * 256, (k4 + 1) * 256), k == 0, k == KT - 1)
                    if s == 1 and t < PT - 1:
                        last.then_inc(tile_done, 1)
                last.then_inc(w_used, 1)
            def turn_in(g):
                if g < 2:
                    pe.wait_ge(v_ok, 4)
                elif g < 6:
                    pe.wait_ge(qn_ok, 4 + g % 4 + 1)
                elif g == 6:
                    pe.wait_ge(qn_ok, 12)
                else:
                    pe.wait_ge(tp_ok, g)
                pe.wait_ge(qrot_ok, 4 if g < 2 else (8 if g < 6 else 12))
                for t in range(PT):
                    src = kd[:, t, g, :, :].rearrange("p i d -> p (i d)") if g < 2 else \
                        qn[:, t, (g - 2) * P:(g - 1) * P]
                    last = nc.tensor.transpose(ps[:, turn_bank(g), t * P:(t + 1) * P], src, ident[:, :])
                last.then_inc(tp_done, 1)

            def scores(g):
                c, n = GROUPS[g]
                if g == 0:
                    pe.wait_ge(tp_ok, 6)
                    pe.wait_ge(cst, 8)
                elif g == 2:
                    pe.wait_ge(qn_ok, 9)
                elif g >= 3:
                    pe.wait_ge(ex_ok, g - 2)
                if n == 0 and c == 1:
                    pe.wait_ge(tp_ok, 10)
                nk = CHUNK if n == 0 else P
                keys = kTe if n % 2 == 0 else kTo
                out4 = ps[:, score_bank(g), :].rearrange("p (par i k) -> p i par k", i=2, k=P)
                for i in range(2):
                    j = 4 * c + 2 * i
                    last = nc.tensor.matmul(out4[:, i, :, 0:nk],
                                            qT[:, n, j:j + 2, :].rearrange("p j q -> p (j q)"),
                                            keys[:, :, c, n // 2, 0:nk], start=True, stop=True)
                last.then_inc(s_done, 1)

            for cb in range(2):
                for s in range(2):
                    unit(PAIR_Q + cb, s)
                    for t in range(PT):
                        if cb == 0 and s == 0:
                            if t == 1:
                                columns(ST_A, SQ_BASE[NORM_A] + KT)
                            if t == 2:
                                pe.wait_ge(var_ok, ST_A + 1)
                        if cb == 1 and s == 0:
                            pe.wait_ge(v_ok, t + 1)
                            pe.wait_ge(qn_ok, t + 1)
                            if t >= 2:
                                pe.wait_ge(tp_ok, PT - t)
                        for k4 in range(4):
                            k = 4 * s + k4
                            last = mm3(ps[:, (0 if cb else 4) + t, :], hidden(k, t * P, (t + 1) * P),
                                       weights(s, k4 * S, (k4 + 1) * S), k == 0, k == KT - 1)
                        if s == 1 and t < PT - 1:
                            last.then_inc(tile_done, 1)
                        if t == PT - 1:
                            last.then_inc(w_used, 1)
                        if cb == 1 and s == 1:
                            if t == 0:
                                for g in range(2, 6):
                                    turn_in(g)
                            else:
                                scores(t - 1)
                        if cb == 0 and s == 1 and t == 2:
                            pe.wait_ge(c_in, 16 * C_DMAS)
                            turn_in(0)
                            turn_in(1)

            def turn(g):
                if g < 2:
                    pe.wait_ge(qn_ok, 10 + g)
                else:
                    pe.wait_ge(pt_ok, g - 1)
                pe.wait_ge(pn_ok, g + 1)
                for i in range(4):
                    last = nc.tensor.transpose(ps[:, probs_bank(g), i * P:(i + 1) * P], pn[:, g % 2, i, :], ident[:, :])
                last.then_inc(pt_done, 1)

            def values(g):
                c, n = GROUPS[g]
                pe.wait_ge(pt_ok, g + 1)
                if g == 0:
                    pe.wait_ge(ve_ok, 2)
                elif g >= 2:
                    pe.wait_ge(alo_ok, g - 1)
                v = ve if n % 2 == 0 else va
                for par in range(2):
                    last = nc.tensor.matmul(ps[par * A_DH:(par + 1) * A_DH, 4 + g % 2, 0:4 * CHUNK],
                                            v[:, n // 2, c * A_DH:(c + 1) * A_DH],
                                            pT[:, g % 2, par * 256:(par + 1) * 256], start=True, stop=True)
                last.then_inc(pv_done, 1)

            NG = len(GROUPS)
            for st in range(NG + 2):
                if st >= 2:
                    values(st - 2)
                if st < NG:
                    turn(st)
                if st == 6:
                    scores(8)
                if st + 3 < NG and st != 5:
                    scores(st + 3)
                if 2 <= st <= 5:
                    turn_in(4 + st)

            for j in range(2):
                for s in range(2):
                    unit(PAIR_WO + j, s)
                    for e in range(2):
                        m = 4 * j + 2 * s + e
                        if m >= 4:
                            pe.wait_ge(xe_ok, XE_WO + m - 3)
                        for k in range(KT):
                            if m == 0 and k % 4 == 0:
                                pe.wait_ge(alo_ok, NCH * (k // 4 + 1))
                            last = mm3(ps[:, m % 4, :], weights(s, (e * KT + k) * P, (e * KT + k + 1) * P),
                                       (a_hi[:, k, :], a_lo[:, k, :]), k == 0, k == KT - 1)
                        last.then_inc(w_used if e else tile_done, 1)

            def mlp(layer):
                up, dn = PAIR_UP[layer], PAIR_DN[layer]
                norm = (NORM_F0, NORM_F1)[layer]

                def up_pair(j, s, first=False):
                    f = FT * layer + 2 * j + s
                    unit(up + j, s)
                    for ab in range(2):
                        if not first:
                            pe.wait_ge(u_ok, 2 * f - 3 + ab)
                        elif layer == 0:
                            pe.wait_ge(xe_ok, XE_WO + 5 + 2 * s + ab)
                        else:
                            pe.wait_ge(pj_ok, KT * R_HEADS - 3 + 2 * s + ab)
                        for k in range(KT):
                            if first and s == 0 and ab == 0:
                                pe.wait_ge(h_ready, KT * norm + k + 1)
                            c = (ab * KT + k) * P
                            last = mm3(ps[:, 2 * s + ab, :], weights(s, c, c + P), hidden(k), k == 0, k == KT - 1)
                            if first and s == 1 and ab == 0 and k == 3:
                                broadcast(ST_F1 if layer else ST_F0, 0)
                        last.then_inc(w_used if ab else tile_done, 1)
                        if first and s == 0 and ab == 1:
                            columns(ST_F1 if layer else ST_F0, SQ_BASE[norm] + KT)

                for s in range(2):
                    up_pair(0, s, first=True)
                with pe.Fori(1, FT // 2) as j:
                    for s in range(2):
                        up_pair(j, s)

                xe = (XE_DN0, XE_DN1)[layer]

                def down(m, e, wait_g=False):
                    if not (isinstance(m, int) and m < 2):
                        pe.wait_ge(xe_ok, xe + m - 1)
                    for s in range(2):
                        unit(dn + m, s)
                        for k11 in range(KH):
                            k = KH * s + k11
                            if wait_g and (k11 == 0 or k >= FT - 2):
                                pe.wait_ge(glo_ok, FT * layer + (KH if s == 0 else max(k + 1, FT - 2)))
                            last = mm3(ps[:, 4 + e, :], weights(s, k11 * P, (k11 + 1) * P),
                                       (g_hi[:, k, :], g_lo[:, k, :]), k == 0, k == FT - 1)
                        last.then_inc(w_used, 1)

                for e in range(2):
                    down(e, e, wait_g=(e == 0))
                with pe.Fori(1, KT // 2) as j:
                    for e in range(2):
                        down(2 * j + e, e)

            mlp(0)

            def qkvg(h, first):
                p0 = PAIR_RET if first else PAIR_RET + 4 * h - 1
                for s in range(2):
                    unit(p0, s)
                    for e in range(2):
                        if not first:
                            pe.wait_ge(gx_ok, 4 * (h - 1) + 2 * s + e + 1)
                        elif s == 0:
                            pe.wait_ge(xe_ok, XE_DN0 + 7 + e)
                        if first and s == 1 and e == 1:
                            pe.wait_ge(bc_ok, BC_R + 1)
                        for k in range(KT):
                            if first and s == 0 and e == 0:
                                pe.wait_ge(h_ready, KT * NORM_R + k + 1)
                            last = mm3(ps[:, 4 + 2 * s + e, :], weights(s, (e * KT + k) * P, (e * KT + k + 1) * P),
                                       hidden(k), k == 0, k == KT - 1)
                        if e == 1:
                            last.then_inc(w_used, 1)
                        if first and s == 0 and e == 0:
                            columns(ST_R, SQ_BASE[NORM_R] + KT)
                        if first and s == 0 and e == 1:
                            broadcast(ST_R, 0)
                        if not first and s == 0 and e == 1:
                            pe.wait_ge(sq_ok, SQ_HEAD + 4 * h)
                            columns(ST_HEAD + h - 1, SQ_HEAD + 4 * h, bank=3)
                        if not first and s == 1 and e == 0:
                            broadcast(ST_HEAD + h - 1, 1, bank=2)
                if not first:
                    project(h - 1, p0 + 1)
                pv = PAIR_RET + 1 if first else p0 + 2
                for s in range(2):
                    unit(pv, s)
                    for t in range(PT):
                        if s == 0 and t % 2 == 0:
                            pe.wait_ge(rt_ok, 4 * h + t + 2)
                        for k4 in range(4):
                            k = 4 * s + k4
                            last = mm3(ps[:, 4 + t, :], hidden(k, t * P, (t + 1) * P),
                                       weights(s, k4 * S, (k4 + 1) * S), k == 0, k == KT - 1)
                    last.then_inc(w_used, 1)
                pe.wait_ge(qlo_ok, 4 * h + 4)
                for t in range(PT):
                    if not first:
                        pe.wait_ge(pj_ok, KT * (h - 1) + 5 + t)
                    for d in range(2):
                        key, query = slice(t * P, (t + 1) * P), slice(t * P, S)
                        last = mm3(ps[:, t, 0:S - t * P], (qk_hi[:, 2 + d, key], qk_lo[:, 2 + d, key]),
                                   (qk_hi[:, d, query], qk_lo[:, d, query]), d == 0, d == 1)
                    last.then_inc(rs_done, 1)
                for s in range(2):
                    unit(pv + 1, s)
                    for e in range(2):
                        m = 2 * s + e
                        pe.wait_ge(vlo_ok, 4 * h + m + 1)
                        for k in range(KT):
                            last = mm3(ps[:, 4 + m, :], weights(s, (e * KT + k) * P, (e * KT + k + 1) * P),
                                       hidden(k), k == 0, k == KT - 1)
                    last.then_inc(w_used, 1)
                pe.wait_ge(plo_ok, 4 * h + 4)
                for m in range(RV_T):
                    for t in range(PT):
                        w = S - t * P
                        last = mm3(ps[:, m, t * P:S], (v_hi[:, t, m * P:(m + 1) * P], v_lo[:, t, m * P:(m + 1) * P]),
                                   (p_hi[:, t, 0:w], p_lo[:, t, 0:w]), t == 0, t == PT - 1)
                    last.then_inc(o_done, 1)

            def project(h, p, last_head=False):
                for s in range(2):
                    unit(p, s)
                    for e in range(4):
                        if last_head and s == 0 and e == 1:
                            pe.wait_ge(sq_ok, SQ_HEAD + 4 * (h + 1))
                            columns(ST_HEAD + h, SQ_HEAD + 4 * (h + 1), bank=3)
                        if not last_head and s == 0 and e == 2:
                            pe.wait_ge(bc_ok, BC_HEAD + h + 1)
                        if last_head and s == 0 and e == 2:
                            pe.wait_ge(gx_ok, 4 * R_HEADS)
                            broadcast(ST_HEAD + h, 1)
                        if s == 0:
                            pe.wait_ge(sq_ok, SQ_HEAD + 4 * h + e + 1)
                        else:
                            pe.wait_ge(pj_ok, KT * h + e + 1)
                        for k in range(RV_T):
                            if s == 0 and e == 0:
                                pe.wait_ge(olo_ok, 4 * h + k + 1)
                            c = (e * RV_T + k) * P
                            last = mm3(ps[:, e, :], weights(s, c, c + P), (o_hi[:, k, :], o_lo[:, k, :]),
                                       k == 0, k == RV_T - 1)
                        last.then_inc(w_used if e == 3 else tile_done, 1)

            qkvg(0, True)
            with pe.Fori(1, R_HEADS) as h:
                qkvg(h, False)
            project(R_HEADS - 1, PAIR_UP[1] - 1, last_head=True)

            mlp(1)


def _tables():
    def angles(base, rot, half):
        inv = (np.float64(np.float32(base)) ** (-np.arange(half) * 2.0 / rot)).astype(np.float32)
        return (np.arange(S, dtype=np.float32)[:, None] * inv[None, :]).astype(np.float64)

    half = A_ROT // 2
    a = angles(ROPE_THETA, A_ROT, half)
    cos, sin = np.cos(a), np.sin(a)
    rot_a = np.stack([np.concatenate([cos, cos], 1), np.concatenate([-sin, sin], 1)])
    rot_a = rot_a.reshape(2, PT, P, A_ROT).transpose(2, 0, 1, 3).astype(np.float32)
    b = angles(R_BASE, R_QK, R_QK // 2)
    rot_r = np.stack([np.cos(b).T, np.sin(b).T], 1).astype(np.float32)
    lg = np.log1p(-np.power(2.0, -5.0 - np.arange(R_HEADS)))
    key, query = np.arange(P)[:, None, None], np.arange(S)[None, None, :]
    decay = np.exp(lg[None, :, None] * np.abs(query - key)) * (query // CHUNK >= key // CHUNK) * R_QK ** -0.5
    return np.eye(P, dtype=np.float32), rot_a, rot_r, decay.astype(np.float32)


def kernel(x, norm1_g, norm2_g, attn_w_qkv, attn_w_o, attn_q_gain, attn_k_gain, attn_sinks,
           ret_w_in, ret_w_o, ffn_w_up, ffn_conv_w, ffn_conv_b, ffn_w_down):
    import concourse.bacc as bacc
    from concourse.bass_utils import run_bass_kernel_spmd

    A = np.asarray
    c = np.ascontiguousarray
    arrays = {}
    arrays["xT"] = c(A(x)[0].T.reshape(KT, P, S))

    def moving(w, cols):
        return w.reshape(2, 4, P, cols).transpose(0, 2, 1, 3).reshape(2, P, 4 * cols)

    def stationary(w, kt, per):
        n = w.shape[1] // P
        return w.reshape(kt, P, n // per, per, P).transpose(2, 1, 3, 0, 4).reshape(n // per, P, per * kt * P)

    wqkv = A(attn_w_qkv)[0]
    arrays["w_kv"] = c(moving(wqkv[:, D:], 256))
    arrays["w_q"] = c(np.concatenate([moving(wqkv[:, 0:S], S), moving(wqkv[:, S:D], S)]))
    arrays["w_ao"] = c(stationary(A(attn_w_o)[0], KT, 2))
    for layer in range(2):
        wu = A(ffn_w_up)[layer].reshape(KT, P, 2, FT, P)
        wu_arr = c(wu.transpose(3, 1, 2, 0, 4).reshape(FT, P, UW))
        wd = A(ffn_w_down)[layer].reshape(2, KH, P, KT, P)
        wd_arr = c(wd.transpose(3, 0, 2, 1, 4).reshape(2 * KT, P, DW))
        arrays[f"w_up{layer}"], arrays[f"w_dn{layer}"] = wu_arr, wd_arr
    wr, wo = A(ret_w_in)[0], A(ret_w_o)[0]
    units = []
    for h in range(R_HEADS + 1):
        if h < R_HEADS:
            units += [stationary(wr[:, i * D + h * R_QK:i * D + (h + 1) * R_QK], KT, 2) for i in range(2)]
        if h > 0:
            units.append(stationary(wo[(h - 1) * R_V:h * R_V], RV_T, 4))
        if h < R_HEADS:
            units.append(moving(wr[:, 2 * D + h * R_V:2 * D + (h + 1) * R_V], R_V))
            units.append(stationary(wr[:, 4 * D + h * R_V:4 * D + (h + 1) * R_V], KT, 2))
    arrays["w_ret"] = c(np.concatenate(units))
    arrays["gains"] = c(np.stack([A(norm1_g)[0], A(norm2_g)[0], A(norm1_g)[1], A(norm2_g)[1]])
                        .reshape(4, KT, P).transpose(2, 0, 1))
    cw = np.concatenate([A(ffn_conv_w)[:, :, 0, :], A(ffn_conv_b)[:, None, :]], 1)
    arrays["conv"] = c(cw.reshape(2, 4, 2, FT, P).transpose(4, 0, 3, 2, 1).reshape(P, 2, FT, 8))
    half = A_ROT // 2
    qk = [A(attn_q_gain)[0], A(attn_k_gain)[0]]
    one = np.ones(A_ROT, np.float32)
    arrays["gain_col"] = c(np.stack([np.concatenate([one, g[A_ROT:]] * 2) for g in qk], 1))
    g_rot = np.stack([np.stack([g[:A_ROT], np.concatenate([g[half:A_ROT], g[:half]])]) for g in qk])
    arrays["gain_rot"] = c(np.broadcast_to(g_rot[None], (P, 2, 2, A_ROT)))
    sk = A(attn_sinks)[0].reshape(A_KVH, 2, 2, 2)
    sk = sk.transpose(2, 0, 3, 1).reshape(2, 1, A_KVH, 4)
    arrays["sinks"] = c(np.broadcast_to(sk, (2, CHUNK, A_KVH, 4)).reshape(P, A_KVH, 4))
    arrays["ident"], arrays["rot_a"], arrays["rot_r"], arrays["decay"] = (c(t) for t in _tables())

    nc = bacc.Bacc("TRN2", target_bir_lowering=False, num_devices=1)
    args = [nc.dram_tensor(f"in_{n}", a.shape, F32, kind="ExternalInput").ap() for n, a in arrays.items()]
    out = nc.dram_tensor("out", (KT, P, S), F32, kind="ExternalOutput").ap()
    names = list(arrays)
    by = dict(zip(names, args))
    trunk(nc, by["xT"], by["w_kv"], by["w_q"], by["w_ao"], by["w_up0"], by["w_dn0"], by["w_ret"], by["w_up1"],
          by["w_dn1"], by["gains"], by["conv"], by["gain_col"], by["gain_rot"], by["sinks"], by["ident"],
          by["rot_a"], by["rot_r"], by["decay"], out)
    r = run_bass_kernel_spmd(nc, [{f"in_{n}": a for n, a in arrays.items()}], core_ids=[0])
    got = r.results[0]["out"]
    return np.ascontiguousarray(got.reshape(D, S).T).reshape(1, S, D)
```
